# Optimizing a Trainium2 kernel written in Bass

```python
import math
import jax, jax.numpy as jnp
from jax import lax
import numpy as np

D_MODEL = 1024
BATCH = 1
SEQ = 128
DEPTH = 2
DEC_BATCH = 1
DEC_SEQ = 256
PAST_LEN = 128

GRID_W = 64
CHUNK = 128
Q_BLOCK = 128
EPS = 1e-6

H_SSD = 8
P_SSD = 64
D_SSD = H_SSD * P_SSD
G_SSD = 2
N_SSD = 64
CONV_W = 5
CONV_DIM = D_SSD + 2 * G_SSD * N_SSD
SSD_PROJ = D_SSD + CONV_DIM + 2 * H_SSD

H_RET = 4
DK_RET = 64
DV_RET = 64
D_RET = H_RET * DV_RET
RET_PROJ = 2 * H_RET * DK_RET + 2 * H_RET * DV_RET

H_MLA = 4
Q_RANK = 256
KV_RANK = 128
NOPE_DIM = 64
ROPE_DIM = 32
V_DIM = 64
D_MLA = H_MLA * V_DIM
MLA_PROJ = Q_RANK + KV_RANK + ROPE_DIM
ROPE_BASE = 10000.0

D_MIX = D_SSD + D_RET + D_MLA
D_IN = SSD_PROJ + RET_PROJ + MLA_PROJ
D_FF = -(-8 * D_MODEL // (3 * 256)) * 256

kernel_name = 'hybrid_ssd_retention_mla_diffusion_step'

def _rmsnorm(x, w):
    xf = x.astype(jnp.float32)
    y = xf * lax.rsqrt(jnp.mean(xf * xf, axis=-1, keepdims=True) + EPS)
    return (y * w.astype(jnp.float32)).astype(x.dtype)

def _modulation(cond, w_ada, b_ada):
    m = jax.nn.silu(cond) @ w_ada + b_ada
    return jnp.split(m[:, None, :], 6, axis=-1)

def _dwconv(x, w, b):
    ch = x.shape[-1]
    y = lax.conv_general_dilated(x, w[:, None, :].astype(x.dtype), window_strides=(1,),
                                 padding=[(CONV_W // 2, CONV_W // 2)],
                                 dimension_numbers=('NWC', 'WIO', 'NWC'), feature_group_count=ch)
    return y + b.astype(x.dtype)

def _chunked_scan(q, k, v, log_a, h0):
    f32 = jnp.float32
    b, L, nh, n = q.shape
    p = v.shape[-1]
    nc = L // CHUNK
    qc = q.astype(f32).reshape(b, nc, CHUNK, nh, n)
    kc = k.astype(f32).reshape(b, nc, CHUNK, nh, n)
    vc = v.astype(f32).reshape(b, nc, CHUNK, nh, p)
    cum = lax.cumsum(log_a.astype(f32).reshape(b, nc, CHUNK, nh), axis=2)
    idx = jnp.arange(CHUNK)
    lower = (idx[:, None] >= idx[None, :])[None, None, :, :, None]
    seg = cum[:, :, :, None, :] - cum[:, :, None, :, :]
    decay = jnp.exp(jnp.where(lower, seg, -jnp.inf))
    scores = jnp.einsum('bcihn,bcjhn->bcijh', qc, kc) * decay
    y_intra = jnp.einsum('bcijh,bcjhp->bcihp', scores, vc)
    to_end = jnp.exp(cum[:, :, -1:, :] - cum)
    chunk_state = jnp.einsum('bclhn,bclh,bclhp->bchnp', kc, to_end, vc)
    chunk_decay = jnp.exp(cum[:, :, -1, :])

    def step(h_prev, inp):
        cs, cd = inp
        return h_prev * cd[..., None, None] + cs, h_prev

    h_fin, h_enter = lax.scan(step, h0.astype(f32),
                              (jnp.swapaxes(chunk_state, 0, 1), jnp.swapaxes(chunk_decay, 0, 1)))
    h_enter = jnp.swapaxes(h_enter, 0, 1)
    y_inter = jnp.einsum('bcihn,bchnp,bcih->bcihp', qc, h_enter, jnp.exp(cum))
    y = (y_intra + y_inter).reshape(b, L, nh, p)
    return y.astype(q.dtype), h_fin.astype(h0.dtype)

def _directional_scan(q, k, v, log_a, h0, reverse):
    if reverse:
        q, k, v, log_a = (jnp.flip(t, axis=1) for t in (q, k, v, log_a))
    y, h = _chunked_scan(q, k, v, log_a, h0)
    if reverse:
        y = jnp.flip(y, axis=1)
    return y, h

def _ssd(u, conv_w, conv_b, dt_bias, a_log, d_skip, norm_w, h0):
    b, L, _ = u.shape
    z = u[..., :D_SSD]
    xbc = jax.nn.silu(_dwconv(u[..., D_SSD:D_SSD + CONV_DIM], conv_w, conv_b))
    xs = xbc[..., :D_SSD].reshape(b, L, H_SSD, P_SSD)
    bm = xbc[..., D_SSD:D_SSD + G_SSD * N_SSD].reshape(b, L, G_SSD, N_SSD)
    cm = xbc[..., D_SSD + G_SSD * N_SSD:].reshape(b, L, G_SSD, N_SSD)
    bh = jnp.repeat(bm, H_SSD // G_SSD, axis=2)
    ch = jnp.repeat(cm, H_SSD // G_SSD, axis=2)
    dt = jax.nn.softplus((u[..., D_SSD + CONV_DIM:].reshape(b, L, 2, H_SSD) + dt_bias).astype(jnp.float32))
    a = -jnp.exp(a_log.astype(jnp.float32))
    y_f, h_f = _directional_scan(ch, bh, xs * dt[:, :, 0, :, None], dt[:, :, 0] * a[0], h0[:, 0], False)
    y_b, h_b = _directional_scan(ch, bh, xs * dt[:, :, 1, :, None], dt[:, :, 1] * a[1], h0[:, 1], True)
    y = (y_f + y_b + d_skip[:, None] * xs).reshape(b, L, D_SSD) * jax.nn.silu(z)
    return _rmsnorm(y.astype(u.dtype), norm_w), jnp.stack([h_f, h_b], axis=1)

def _retention(u, decay_logit, gn_w, h0):
    b, L, _ = u.shape
    nq = H_RET * DK_RET
    q = u[..., :nq].reshape(b, L, H_RET, DK_RET)
    k = u[..., nq:2 * nq].reshape(b, L, H_RET, DK_RET) * (DK_RET ** -0.5)
    v = u[..., 2 * nq:2 * nq + D_RET].reshape(b, L, H_RET, DV_RET)
    g = u[..., 2 * nq + D_RET:]
    log_gamma = jax.nn.log_sigmoid(decay_logit.astype(jnp.float32))
    o_f, s_f = _directional_scan(q, k, v, jnp.broadcast_to(log_gamma[0], (b, L, H_RET)), h0[:, 0], False)
    o_b, s_b = _directional_scan(q, k, v, jnp.broadcast_to(log_gamma[1], (b, L, H_RET)), h0[:, 1], True)
    of = (o_f + o_b).astype(jnp.float32)
    mu = jnp.mean(of, axis=-1, keepdims=True)
    var = jnp.mean(jnp.square(of - mu), axis=-1, keepdims=True)
    on = ((of - mu) * lax.rsqrt(var + EPS)).reshape(b, L, D_RET) * gn_w.astype(jnp.float32)
    return (jax.nn.silu(g) * on).astype(u.dtype), jnp.stack([s_f, s_b], axis=1)

def _axial_rope(n_tokens):
    n_rows = n_tokens // GRID_W
    row, col = jnp.meshgrid(jnp.arange(n_rows), jnp.arange(GRID_W), indexing='ij')
    row = row.reshape(-1).astype(jnp.float32)
    col = col.reshape(-1).astype(jnp.float32)
    half = ROPE_DIM // 2
    inv = ROPE_BASE ** (-jnp.arange(0, half, 2, dtype=jnp.float32) / half)
    ang_r = row[:, None] * inv
    ang_c = col[:, None] * inv
    ang = jnp.concatenate([ang_r, ang_r, ang_c, ang_c], axis=-1)
    return jnp.cos(ang), jnp.sin(ang)

def _rot_half(t):
    t1, t2 = jnp.split(t, 2, axis=-1)
    return jnp.concatenate([-t2, t1], axis=-1)

def _apply_rope(x, cos, sin):
    xr, xc = jnp.split(x, 2, axis=-1)
    rot = jnp.concatenate([_rot_half(xr), _rot_half(xc)], axis=-1)
    out = x.astype(jnp.float32) * cos[:, None, :] + rot.astype(jnp.float32) * sin[:, None, :]
    return out.astype(x.dtype)

def _block_attention(q, k, v):
    b, L, nh, dq = q.shape
    nb = L // Q_BLOCK
    qb = jnp.swapaxes(q.reshape(b, nb, Q_BLOCK, nh, dq), 0, 1)
    scale = dq ** -0.5

    def one_block(qblk):
        s = jnp.einsum('bqhd,bkhd->bhqk', qblk, k).astype(jnp.float32) * scale
        p = jax.nn.softmax(s, axis=-1)
        return jnp.einsum('bhqk,bkhd->bqhd', p.astype(v.dtype), v)

    o = lax.map(one_block, qb)
    return jnp.swapaxes(o, 0, 1).reshape(b, L, nh, v.shape[-1])

def _mla(u, q_norm_w, w_uq, kv_norm_w, w_ukv, rope, ctx_kv):
    b, L, _ = u.shape
    q_c = _rmsnorm(u[..., :Q_RANK], q_norm_w)
    ckv = _rmsnorm(u[..., Q_RANK:Q_RANK + KV_RANK], kv_norm_w)
    krope = u[..., Q_RANK + KV_RANK:]
    q = (q_c @ w_uq).reshape(b, L, H_MLA, NOPE_DIM + ROPE_DIM)
    q_nope, q_rope = q[..., :NOPE_DIM], q[..., NOPE_DIM:]
    if ctx_kv is None:
        ckv_all, kr_all = ckv, krope
    else:
        cos, sin = rope
        q_rope = _apply_rope(q_rope, cos, sin)
        kr_lat = _apply_rope(krope[:, :, None, :], cos, sin)[:, :, 0]
        ckv_all = jnp.concatenate([ctx_kv[0].astype(ckv.dtype), ckv], axis=1)
        kr_all = jnp.concatenate([ctx_kv[1].astype(kr_lat.dtype), kr_lat], axis=1)
    s_len = ckv_all.shape[1]
    kv = (ckv_all @ w_ukv).reshape(b, s_len, H_MLA, NOPE_DIM + V_DIM)
    k = jnp.concatenate([kv[..., :NOPE_DIM],
                         jnp.broadcast_to(kr_all[:, :, None, :], (b, s_len, H_MLA, ROPE_DIM)).astype(kv.dtype)], axis=-1)
    v = kv[..., NOPE_DIM:]
    o = _block_attention(jnp.concatenate([q_nope, q_rope], axis=-1), k, v)
    return o.reshape(b, L, D_MLA), ckv, krope

def _layer(x, cond, lp, ctx, rope):
    b = x.shape[0]
    sh1, sc1, g1, sh2, sc2, g2 = _modulation(cond, lp['w_ada'], lp['b_ada'])
    h = _rmsnorm(x, lp['norm1_w']) * (1 + sc1) + sh1
    u = h @ lp['w_in']
    u_ssd = u[..., :SSD_PROJ]
    u_ret = u[..., SSD_PROJ:SSD_PROJ + RET_PROJ]
    u_mla = u[..., SSD_PROJ + RET_PROJ:]
    if ctx is None:
        ssd_h0 = jnp.zeros((b, 2, H_SSD, N_SSD, P_SSD), x.dtype)
        ret_h0 = jnp.zeros((b, 2, H_RET, DK_RET, DV_RET), x.dtype)
        ctx_kv = None
    else:
        ssd_h0, ret_h0, ckv_ctx, kr_ctx = ctx
        ctx_kv = (ckv_ctx, kr_ctx)
    y_ssd, ssd_state = _ssd(u_ssd, lp['ssd_conv_w'], lp['ssd_conv_b'], lp['ssd_dt_bias'], lp['ssd_A_log'],
                            lp['ssd_D'], lp['ssd_norm_w'], ssd_h0)
    y_ret, ret_state = _retention(u_ret, lp['ret_decay_logit'], lp['ret_gn_w'], ret_h0)
    y_mla, ckv, krope = _mla(u_mla, lp['mla_q_norm_w'], lp['mla_w_uq'], lp['mla_kv_norm_w'], lp['mla_w_ukv'],
                             rope, ctx_kv)
    mix = jnp.concatenate([y_ssd.astype(x.dtype), y_ret.astype(x.dtype), y_mla.astype(x.dtype)], axis=-1)
    x = x + g1 * (mix @ lp['w_out'])
    h2 = _rmsnorm(x, lp['norm2_w']) * (1 + sc2) + sh2
    a, gt = jnp.split(h2 @ lp['ffn_w1'], 2, axis=-1)
    x = x + g2 * ((jax.nn.silu(a) * gt) @ lp['ffn_w2'])
    return x, (ssd_state, ret_state, ckv, krope)

def setup_inputs(seed: int = 0) -> dict:
    key = jax.random.key(seed)
    ks = jax.random.split(key, 32)
    f32 = jnp.float32

    def nrm(i, shape, scale):
        return jax.random.normal(ks[i], shape, f32) * scale

    def gain(i, shape):
        return 1.0 + nrm(i, shape, 0.02)

    dt0 = jnp.exp(jax.random.uniform(ks[14], (DEPTH, 2, H_SSD), f32, math.log(1e-3), math.log(1e-1)))
    ret_base = jnp.log(2.0 ** (5.0 + jnp.arange(H_RET, dtype=f32)) - 1.0)
    return {
        'x_prompt': nrm(0, (BATCH, SEQ, D_MODEL), 1.0),
        'x_sample': nrm(1, (DEC_BATCH, DEC_SEQ, D_MODEL), 1.0),
        'c': nrm(2, (DEC_BATCH, D_MODEL), 1.0),
        'state_ssd': nrm(3, (DEC_BATCH, DEPTH, 2, H_SSD, N_SSD, P_SSD), 0.5),
        'state_ret': nrm(4, (DEC_BATCH, DEPTH, 2, H_RET, DK_RET, DV_RET), 0.5),
        'cache_mla_ckv': nrm(5, (DEC_BATCH, DEPTH, PAST_LEN, KV_RANK), 1.0),
        'cache_mla_krope': nrm(6, (DEC_BATCH, DEPTH, PAST_LEN, ROPE_DIM), 1.0),
        'c_ctx': nrm(7, (D_MODEL,), 1.0),
        'w_ada': nrm(8, (DEPTH, D_MODEL, 6 * D_MODEL), 0.5 * D_MODEL ** -0.5),
        'b_ada': nrm(9, (DEPTH, 6 * D_MODEL), 0.01),
        'norm1_w': gain(10, (DEPTH, D_MODEL)),
        'w_in': nrm(11, (DEPTH, D_MODEL, D_IN), D_MODEL ** -0.5),
        'ssd_conv_w': nrm(12, (DEPTH, CONV_W, CONV_DIM), CONV_W ** -0.5),
        'ssd_conv_b': nrm(13, (DEPTH, CONV_DIM), 0.01),
        'ssd_dt_bias': dt0 + jnp.log(-jnp.expm1(-dt0)),
        'ssd_A_log': jnp.log(jax.random.uniform(ks[15], (DEPTH, 2, H_SSD), f32, 1.0, 16.0)),
        'ssd_D': gain(16, (DEPTH, H_SSD)),
        'ssd_norm_w': gain(17, (DEPTH, D_SSD)),
        'ret_decay_logit': ret_base + nrm(18, (DEPTH, 2, H_RET), 0.1),
        'ret_gn_w': gain(19, (DEPTH, D_RET)),
        'mla_q_norm_w': gain(20, (DEPTH, Q_RANK)),
        'mla_w_uq': nrm(21, (DEPTH, Q_RANK, H_MLA * (NOPE_DIM + ROPE_DIM)), Q_RANK ** -0.5),
        'mla_kv_norm_w': gain(22, (DEPTH, KV_RANK)),
        'mla_w_ukv': nrm(23, (DEPTH, KV_RANK, H_MLA * (NOPE_DIM + V_DIM)), KV_RANK ** -0.5),
        'w_out': nrm(24, (DEPTH, D_MIX, D_MODEL), D_MIX ** -0.5),
        'norm2_w': gain(25, (DEPTH, D_MODEL)),
        'ffn_w1': nrm(26, (DEPTH, D_MODEL, 2 * D_FF), D_MODEL ** -0.5),
        'ffn_w2': nrm(27, (DEPTH, D_FF, D_MODEL), D_FF ** -0.5),
        'final_norm_w': gain(28, (D_MODEL,)),
    }

def reference(x_prompt, x_sample, c, state_ssd, state_ret, cache_mla_ckv, cache_mla_krope, c_ctx,
              w_ada, b_ada, norm1_w, w_in, ssd_conv_w, ssd_conv_b, ssd_dt_bias, ssd_A_log, ssd_D, ssd_norm_w,
              ret_decay_logit, ret_gn_w, mla_q_norm_w, mla_w_uq, mla_kv_norm_w, mla_w_ukv, w_out, norm2_w,
              ffn_w1, ffn_w2, final_norm_w):
    stacked = dict(w_ada=w_ada, b_ada=b_ada, norm1_w=norm1_w, w_in=w_in, ssd_conv_w=ssd_conv_w,
                   ssd_conv_b=ssd_conv_b, ssd_dt_bias=ssd_dt_bias, ssd_A_log=ssd_A_log, ssd_D=ssd_D,
                   ssd_norm_w=ssd_norm_w, ret_decay_logit=ret_decay_logit, ret_gn_w=ret_gn_w,
                   mla_q_norm_w=mla_q_norm_w, mla_w_uq=mla_w_uq, mla_kv_norm_w=mla_kv_norm_w,
                   mla_w_ukv=mla_w_ukv, w_out=w_out, norm2_w=norm2_w, ffn_w1=ffn_w1, ffn_w2=ffn_w2)

    xp = x_prompt
    cond_ctx = c_ctx[None, :]
    ssd_list, ret_list, ckv_list, kr_list = [], [], [], []
    for i in range(DEPTH):
        lp = {name: arr[i] for name, arr in stacked.items()}
        xp, (s_ssd, s_ret, ckv, kr) = _layer(xp, cond_ctx, lp, None, None)
        ssd_list.append(s_ssd)
        ret_list.append(s_ret)
        ckv_list.append(ckv)
        kr_list.append(kr)
    y_prompt = _rmsnorm(xp, final_norm_w)

    rope = _axial_rope(x_sample.shape[1])
    xs = x_sample
    for i in range(DEPTH):
        lp = {name: arr[i] for name, arr in stacked.items()}
        ctx = (state_ssd[:, i], state_ret[:, i], cache_mla_ckv[:, i], cache_mla_krope[:, i])
        xs, _ = _layer(xs, c, lp, ctx, rope)
    y_sample = _rmsnorm(xs, final_norm_w)

    return (y_prompt, y_sample, jnp.stack(ssd_list, axis=1), jnp.stack(ret_list, axis=1),
            jnp.stack(ckv_list, axis=1), jnp.stack(kr_list, axis=1))


_drawn_inputs = setup_inputs


def setup_inputs(seed=0):
    import zlib

    import numpy as np

    out = dict(_drawn_inputs(seed))
    spreads = {}
    factors = {'cache_mla_ckv': 5.228,
     'cache_mla_krope': 8.0,
     'ssd_conv_b': 3.21,
     'ssd_D': 8.0,
     'ssd_norm_w': 8.0,
     'ret_gn_w': 8.0,
     'mla_q_norm_w': 8.0,
     'mla_kv_norm_w': 3.14,
     'norm2_w': 6.452,
     'final_norm_w': 2.732}
    for name, (base, spread) in spreads.items():
        noise = np.random.default_rng([zlib.crc32(name.encode()), seed]).standard_normal(out[name].shape)
        drawn = base * np.exp(spread * noise) if base else spread * noise
        out[name] = __import__('jax').numpy.asarray(drawn.astype(out[name].dtype))
    for name, factor in factors.items():
        out[name] = (out[name] * factor).astype(out[name].dtype)
    return out
```

```python
from contextlib import ExitStack

import numpy as np

import concourse.bass as bass
from concourse import mybir

F32 = mybir.dt.float32
F32R = mybir.dt.float32r
ALU = mybir.AluOpType
ACT = mybir.ActivationFunctionType
AX_X = mybir.AxisListType.X

P = 128
D = 1024
KD = D // P
DEPTH = 2
CTX, LAT = 128, 256
T = CTX + LAT
NCH = T // P
EPS = 1e-6
HS, HSG, NS = 8, 4, 64
HR, HM = 4, 4
RANKQ, RANKKV, ROPE, NOPE = 256, 128, 32, 64
DFF = 2816
KF = DFF // P
KH2 = KF // 2
SCALE = float(NOPE + ROPE) ** -0.5
CONVW = 5
PADT = T + 8
CONVT = T + 4
CS = (0, 132, 260)
LATC = CS[1]

BLK = KD * 2 * P
N_WIN, N_WOUT, N_F1, N_F2 = 12, 4, KF, 2 * KD
F2BLK = KH2 * P
NB = N_WIN + N_WOUT + N_F1 + N_F2
ADA_PAIRS = 12
FILLS = 4

def columns(*widths):
    return np.concatenate([[0], np.cumsum(widths)]).tolist()


(C_N1, C_N2, C_CW, C_CB, C_SN, C_GN, C_QN, C_KN, C_DSK, C_DTB, C_ALOG, C_LGB, C_LGC, C_H0S, C_H0R, C_CKV, C_KR,
 C_UQ, C_UKV, SMALLW) = columns(KD, KD, CONVW * 6, 6, 4, 2, 2, 1, 4, 16, 16, 8, 4, 512, 256, P, P, 768, 512)
(K_ID, K_U, K_L, K_SU, K_SL, K_BD, K_ONE, K_PF, K_PB, K_IP, K_IB, K_COS, K_SIN, K_PERM, K_PC, K_EPS, K_BADA, K_FN,
 K_COND, CONSTW) = columns(*[P] * 11, LAT, LAT, NOPE + ROPE, 2, 1, DEPTH * 48, KD, 2 * KD)

U_RQ, U_RK, U_RV, U_MQ, U_CKV, U_KR, U_Z, U_G = 0, 2, 4, 6, 8, 9, 10, 14
KR0 = NOPE

DVE_STEPS = 75
RSTD = 6
ATT = [(c, h) for c in range(NCH) for h in range(HM)]
NATT = len(ATT)


def program(nc, x_d, const_d, small_d, win_d, wdt_d, wout_d, wf1_d, wf2_d, wada_d, y_d, sssd_d, sret_d, ckv_d, kr_d):
    with ExitStack() as ctx:
        def sb(name, shape, dt=F32, stack=ctx):
            return stack.enter_context(nc.sbuf_tensor(name, shape, dt))

        def sem(name):
            return ctx.enter_context(nc.semaphore(name))

        stage_in0 = sem("stage_in0")
        stage_in1 = sem("stage_in1")
        ada_in0 = sem("ada_in0")
        ada_in1 = sem("ada_in1")
        const_in = sem("const_in")
        x_in = sem("x_in")
        small_in = sem("small_in")
        w_hi = sem("w_hi")
        w_split = sem("w_split")
        w_used = sem("w_used")
        ada_used = sem("ada_used")
        mod_ready = sem("mod_ready")
        cond_ready = sem("cond_ready")
        fact1 = sem("fact1")
        fact2 = sem("fact2")
        sq_ready = sem("sq_ready")
        gsq_ready = sem("gsq_ready")
        ms_ready = sem("ms_ready")
        ln_ready = sem("ln_ready")
        y0_ready = sem("y0_ready")
        rstd_ready = sem("rstd_ready")
        xn_ready = sem("xn_ready")
        h_whole = sem("h_whole")
        h_hi_ready = sem("h_hi_ready")
        h_ready = sem("h_ready")
        u_ready = sem("u_ready")
        conv_ready = sem("conv_ready")
        v_ready = sem("v_ready")
        dt_taken = sem("dt_taken")
        abs_ready = sem("abs_ready")
        exps_ready = sem("exps_ready")
        loga_ready = sem("loga_ready")
        cum_ps = sem("cum_ps")
        cum_ready = sem("cum_ready")
        tedt_ready = sem("tedt_ready")
        tr_ps = sem("tr_ps")
        tr_ready = sem("tr_ready")
        vte_ready = sem("vte_ready")
        st_ps = sem("st_ps")
        ssd_state = sem("ssd_state")
        score_ps = sem("score_ps")
        stm_ready = sem("stm_ready")
        row_ps = sem("row_ps")
        ec_ready = sem("ec_ready")
        qsc_ready = sem("qsc_ready")
        seg_ready = sem("seg_ready")
        e_ready = sem("e_ready")
        prob_ready = sem("prob_ready")
        vd_ready = sem("vd_ready")
        y_ps = sem("y_ps")
        ssd_y = sem("ssd_y")
        gates_ready = sem("gates_ready")
        ssd_gated = sem("ssd_gated")
        rexp_ready = sem("rexp_ready")
        rmat_ready = sem("rmat_ready")
        kv_ps = sem("kv_ps")
        kv_ready = sem("kv_ready")
        rvt_ready = sem("rvt_ready")
        rst_ps = sem("rst_ps")
        ret_state = sem("ret_state")
        rscore_ps = sem("rscore_ps")
        rprob_ready = sem("rprob_ready")
        qr_ready = sem("qr_ready")
        ry_ps = sem("ry_ps")
        ry_taken = sem("ry_taken")
        mu_ps = sem("mu_ps")
        centred = sem("centred")
        qn_ready = sem("qn_ready")
        ck_ready = sem("ck_ready")
        krot_ps = sem("krot_ps")
        kr_ready = sem("kr_ready")
        kh_rope = sem("kh_rope")
        q_ps = sem("q_ps")
        q_taken = sem("q_taken")
        rot_ps = sem("rot_ps")
        q_ready = sem("q_ready")
        k_ps = sem("k_ps")
        k_ready = sem("k_ready")
        vm_ps = sem("vm_ps")
        vm_ready = sem("vm_ready")
        s_ps = sem("s_ps")
        max_ready = sem("max_ready")
        p_exp = sem("p_exp")
        p_ready = sem("p_ready")
        pt_ps = sem("pt_ps")
        pt_ready = sem("pt_ready")
        my_ps = sem("my_ps")
        mix_src = sem("mix_src")
        mix_hi = sem("mix_hi")
        mix_ready = sem("mix_ready")
        x_ready = sem("x_ready")
        silu_ready = sem("silu_ready")
        hid_ready = sem("hid_ready")
        hid_hi_ready = sem("hid_hi_ready")
        hid_lo_ready = sem("hid_lo_ready")
        y_ready = sem("y_ready")
        dve_step = sem("dve_step")
        stored = sem("stored")
        stage_in, ada_in = (stage_in0, stage_in1), (ada_in0, ada_in1)

        x = sb("x", [P, KD, T])
        h_hi, h_lo = sb("h_hi", [P, KD, T], F32R), sb("h_lo", [P, KD, T], F32R)
        stage = sb("stage", [P, 2, BLK])
        whi, wlo = sb("whi", [P, 2, BLK], F32R), sb("wlo", [P, 2, BLK], F32R)
        adas = sb("adas", [P, 2, BLK])
        small = sb("small", [P, SMALLW])
        const = sb("const", [P, CONSTW])
        cond = sb("cond", [P, KD, 2])
        mod = sb("mod", [P, DEPTH * 48, 2])
        modl = sb("modl", [P, 48, 2])
        nv, ny, nt = (sb(n, [P, 2, T]) for n in ("nv", "ny", "nt"))
        upad = sb("upad", [P, 6, PADT])
        ps = ctx.enter_context(nc.psum_tensor("ps", [P, 8, 512], F32))

        with ExitStack() as region:
            hid_hi, hid_lo = (sb(n, [P, KF, T], F32R, region) for n in ("hid_hi", "hid_lo"))
        with ExitStack() as region:
            sq = sb("sq", [P, KD, T], F32, region)
        with ExitStack() as region:
            u = sb("u", [P, 16, T], F32, region)
            bt = sb("bt", [P, NCH, P], F32, region)
            dts = sb("dts", [P, 60], F32, region)
            spx, spp, sps, spq = (sb(n, [P, 60], F32, region) for n in ("spx", "spp", "sps", "spq"))
            loga = sb("loga", [P, NCH, 2, HS], F32, region)
            expa = sb("expa", [P, 16], F32, region)
            lg = sb("lg", [P, 12], F32, region)
            cum = sb("cum", [P, 2, NCH, HS], F32, region)
            tedt = sb("tedt", [P, 2, NCH, HS], F32, region)
            cd = sb("cd", [P, 2, HSG], F32, region)
            hs = sb("hs", [P, 2, 256], F32, region)
            hr = sb("hr", [P, 2, 2, 64], F32, region)
            sout = sb("sout", [P, 2, 256], F32, region)
            rout = sb("rout", [P, 2, 2, 64], F32, region)
            att = sb("att", [P, 4, NATT], F32, region)
            with ExitStack() as part:
                v = sb("v", [P, 6, CONVT], F32, part)
                xt = sb("xt", [P, NCH, 512], F32, part)
                vd = sb("vd", [P, 2, 512], F32, part)
                vte = sb("vte", [P, 512], F32, part)
                ew = sb("ew", [P, 2, HSG, P], F32, part)
                stm = sb("stm", [P, 2, 2, P], F32, part)
                ec = sb("ec", [P, 2, HSG, P], F32, part)
            with ExitStack() as part:
                kvt = sb("kvt", [P, NCH, 512], F32, part)
                rmt = sb("rmt", [P, 2, HR, P], F32, part)
                rm = sb("rm", [P, 2, 2, P], F32, part)
                rq = sb("rq", [P, 2, 2, P], F32, part)
                rp = sb("rp", [P, 2, 2, P], F32, part)
                qr = sb("qr", [P, 2, 2, P], F32, part)
                vtr = sb("vtr", [P, 256], F32, part)
                ter = sb("ter", [P, 2, HR], F32, part)
                cdr = sb("cdr", [P, 4], F32, part)
                ry = sb("ry", [P, 2, T], F32, part)
                ry2 = sb("ry2", [P, 2, T], F32, part)
            with ExitStack() as part:
                ck = sb("ck", [P, 512], F32, part)
                kr = sb("kr", [P, 512], F32, part)
                rt = sb("rt", [P, 2, LAT], F32, part)
                qh = sb("qh", [P, HM, T], F32, part)
                kh = sb("kh", [P, HM, 512], F32, part)
                vm = sb("vm", [P, 4, 256], F32, part)
                pr = sb("pr", [P, 2, T], F32, part)
                pt = sb("pt", [P, 2, T], F32, part)

        def cc(k, n=P):
            return const[:, k:k + n]

        def sc(k, n=1):
            return small[:, k:k + n]

        def spread(ap, n, shape):
            return ap.unsqueeze(len(shape)).to_broadcast([P, *shape[1:], n])

        def over(ap, n):
            return ap.unsqueeze(1).to_broadcast([ap.shape[0], n, ap.shape[1]])

        ident, ones = cc(K_ID), cc(K_ONE)
        tri = (cc(K_U), cc(K_L))
        after = (cc(K_SL), cc(K_SU))
        eps = cc(K_EPS, 1)
        STATE_JOBS = ((0, 0), (0, 1), (1, 0), (2, 1))

        def fills(eng, L, f, work):
            with eng.Fori(0, 3 - L) as i:
                work(nc.s_assert_within((12 - f) * L + i + (4 + 3 * f), 4, ADA_PAIRS * DEPTH - 1,
                                        skip_runtime_bounds_check_because="the last layer does one pair less"))

        block = ctx.enter_context(nc.Block())

        @block.sync
        def _(sp):
            def load_ada(pair):
                for j in range(2):
                    sp.wait_ge(ada_used, pair * 2 + (j + 1))
                    sp.dma_start(adas[:, j, :], wada_d[pair * 2 + j]).then_inc(ada_in[j], 16)

            def load_w(L, n, j, dst, src):
                sp.wait_ge(w_split, L * NB + n + 1)
                sp.dma_start(dst, src).then_inc(stage_in[j], 16)

            sp.dma_start(const[:], const_d).then_inc(const_in, 16)
            sp.dma_start(x[:], x_d).then_inc(x_in, 16)
            with sp.Fori(0, 4) as pair:
                load_ada(pair)
            with sp.Fori(0, DEPTH) as L:
                sp.wait_ge(x_ready, L * 16 + 1)
                sp.dma_start(small[:], small_d[L]).then_inc(small_in, 16)
                load_w(L, 0, 0, stage[:, 0, 0:P], wdt_d[L])
                for n in range(1, N_WIN):
                    load_w(L, n, n % 2, stage[:, n % 2, :], win_d[L * (N_WIN - 1) + (n - 1)])
                for i in range(2):
                    load_w(L, N_WIN + i, i, stage[:, i, :], wout_d[L * N_WOUT + i])
                fills(sp, L, 0, load_ada)
                fills(sp, L, 1, load_ada)
                sp.wait_ge(ssd_state, L * 4 + 2)
                sp.dma_start(sssd_d[L], sout[:].rearrange("p a b -> p (a b)")).then_inc(stored, 16)
                fills(sp, L, 2, load_ada)
                fills(sp, L, 3, load_ada)
                sp.wait_ge(ret_state, L * 4 + 2)
                sp.dma_start(sret_d[L], rout[:].rearrange("p a b c -> p (a b c)")).then_inc(stored, 16)
                sp.wait_ge(ck_ready, L * 3 + 3)
                sp.dma_start(ckv_d[L], ck[:, 0:CTX]).then_inc(stored, 16)
                sp.dma_start(kr_d[L], u[KR0:KR0 + ROPE, U_KR, 0:CTX]).then_inc(stored, 16)
                for i in range(2, N_WOUT):
                    load_w(L, N_WIN + i, i % 2, stage[:, i % 2, :], wout_d[L * N_WOUT + i])
                with sp.Fori(0, N_F1 // 2) as i:
                    for j in range(2):
                        load_w(L, i * 2 + (j + N_WIN + N_WOUT), j, stage[:, j, :], wf1_d[L * N_F1 + i * 2 + j])
                with sp.Fori(0, N_F2 // 2) as i:
                    for j in range(2):
                        load_w(L, i * 2 + (j + N_WIN + N_WOUT + N_F1), j, stage[:, j, 0:F2BLK],
                               wf2_d[L * N_F2 + i * 2 + j])
            for half in range(2):
                sp.wait_ge(y_ready, 4 * half + 4)
                sp.dma_start(y_d[:, 4 * half:4 * half + 4, :], sq[:, 4 * half:4 * half + 4, :]).then_inc(stored, 16)
            sp.wait_ge(stored, 16 * (4 * DEPTH + 2))

        @block.tensor
        def _(pe):
            mm, tp = nc.tensor.matmul, nc.tensor.transpose

            def split_mm(out, lhs, rhs, k, n):
                (ah, al), (bh, bl) = lhs, rhs
                mm(out, ah, bh, start=(k == 0), stop=False)
                mm(out, ah, bl, start=False, stop=False)
                return mm(out, al, bh, start=False, stop=(k == n - 1))

            def wtile(j, t):
                return whi[:, j, t * P:(t + 1) * P], wlo[:, j, t * P:(t + 1) * P]

            def hk(k, a=0, b=T):
                return h_hi[:, k, a:b], h_lo[:, k, a:b]

            def w_ready(L, n):
                pe.wait_ge(w_split, L * NB + n + 3)

            def wide_block(L, n, j):
                w_ready(L, n)
                for s in range(2):
                    for k in range(KD):
                        last = split_mm(ps[:, 2 * j + s, 0:T], wtile(j, 2 * k + s), hk(k), k, KD)
                last.then_inc(w_used, 1)

            def ada_pair(pair):
                pe.wait_ge(mod_ready, pair + 1)
                for j in range(2):
                    pe.wait_ge(ada_in[j], pair * 16 + 16)
                    for s in range(2):
                        for k in range(KD):
                            t = 2 * k + s
                            last = mm(ps[:, 4, 4 * j + 2 * s:4 * j + 2 * s + 2], adas[:, j, t * P:(t + 1) * P],
                                      cond[:, k, :], start=(k == 0), stop=(k == KD - 1))
                    last.then_inc(ada_used, 1)

            def mean_square(first):
                for k in range(KD):
                    pe.wait_ge(sq_ready, first + (k + 1))
                    last = mm(ps[:, 7, 0:T], ones, sq[:, k, :], start=(k == 0), stop=(k == KD - 1))
                last.then_inc(ms_ready, 1)

            pe.sem_inc(w_used, 2)
            pe.sem_inc(ada_used, 2)
            pe.wait_ge(cond_ready, 1)
            with pe.Fori(0, 4) as pair:
                ada_pair(pair)

            with pe.Fori(0, DEPTH) as L:
                mean_square(L * 16)

                w_ready(L, 0)
                pe.wait_ge(h_ready, L * 16 + KD)
                for c in range(NCH):
                    for k in range(KD):
                        last = split_mm(ps[:, 0, c * 16:c * 16 + 16], hk(k, c * P, c * P + P),
                                        (whi[:, 0, k * 16:k * 16 + 16], wlo[:, 0, k * 16:k * 16 + 16]), k, KD)
                last.then_inc(w_used, 1)
                for n in range(1, N_WIN):
                    if n == 2:
                        pe.wait_ge(dt_taken, L + 1)
                    if n >= 3:
                        pe.wait_ge(u_ready, L * (N_WIN - 1) + n - 2)
                    wide_block(L, n, n % 2)

                fills(pe, L, 0, ada_pair)

                pe.wait_ge(loga_ready, L * 2 + 2)
                for d in range(2):
                    mm(ps[:, 5, d * 24:d * 24 + 24], tri[d], loga[:, :, d, :], start=True, stop=True)
                    mm(ps[:, 5, 48 + d * 24:72 + d * 24], after[d], loga[:, :, d, :], start=True, stop=True)
                for c, d in STATE_JOBS[2:]:
                    for g in range(2):
                        last = mm(ps[g * 64:g * 64 + 64, 5, 96 + d * 4:100 + d * 4], ones[:, 0:64],
                                  loga[:, c, d, g * 4:g * 4 + 4], start=True, stop=True)
                last.then_inc(cum_ps, 1)

                pe.wait_ge(v_ready, L * 6 + 6)
                pe.wait_ge(cum_ready, L * 3 + 3)
                for c in range(NCH):
                    for t in range(4):
                        last = tp(ps[:, 5 + c, t * P:t * P + P], v[:, t, CS[c]:CS[c] + P], ident)
                    last.then_inc(tr_ps, 1)
                pe.wait_ge(tr_ready, L * 4 + 1)
                for c in range(NCH):
                    last = tp(ps[:, 5, c * P:c * P + P], v[:, 4, CS[c]:CS[c] + P], ident)
                last.then_inc(tr_ps, 1)

                pe.wait_ge(tr_ready, L * 4 + 4)
                for s, (c, d) in enumerate(STATE_JOBS):
                    pe.wait_ge(vte_ready, L * 4 + s + 1)
                    if s >= 2:
                        pe.wait_ge(ssd_state, L * 4 + s - 1)
                    for g in range(2):
                        last = mm(ps[g * 64:g * 64 + 64, 6 + s % 2, 0:256], bt[:, c, g * 64:g * 64 + 64],
                                  vte[:, g * 256:g * 256 + 256], start=True, stop=True)
                    last.then_inc(st_ps, 1)

                fills(pe, L, 1, ada_pair)

                pe.wait_ge(ssd_state, L * 4 + 4)
                pe.wait_ge(u_ready, L * (N_WIN - 1) + N_WIN - 1)
                for c in range(NCH):
                    for g in range(2):
                        q = 2 * c + g
                        rows = slice(g * 64, g * 64 + 64)
                        if q:
                            pe.wait_ge(stm_ready, L * 12 + 2 * q)
                        mm(ps[:, 7, 0:P], v[rows, 4, CS[c]:CS[c] + P], v[rows, 5, CS[c]:CS[c] + P],
                           start=True, stop=True).then_inc(score_ps, 1)
                        if q:
                            pe.wait_ge(seg_ready, L * 6 + q)
                        if q >= 3:
                            pe.wait_ge(ec_ready, L * 4 + q - 2)
                        for d in range(2):
                            for hh in range(HSG):
                                h = g * HSG + hh
                                last = mm(ps[:, 5 + d, hh * P:hh * P + P],
                                          loga[:, c, d, h:h + 1].to_broadcast([P, P]), tri[d], start=True, stop=True)
                        last.then_inc(row_ps, 1)
                        pe.wait_ge(vd_ready, L * 6 + 2 * c + 2)
                        if c:
                            pe.wait_ge(qsc_ready, L * 4 + q - 1)
                        pe.wait_ge(prob_ready, L * 12 + 2 * q + 2)
                        for hh in range(HSG):
                            h = g * HSG + hh
                            o = (h % 2) * 64
                            out = ps[o:o + 64, h // 2, c * P:c * P + P]
                            for d in range(2):
                                last = mm(out, vd[:, d, h * 64:h * 64 + 64], ew[:, d, hh, :], start=(d == 0),
                                          stop=(d == 1 and c == 0))
                            if c:
                                for d in range(2):
                                    if (c, d) in ((1, 0), (2, 1)):
                                        st = small[rows, C_H0S + d * 256 + hh * 64:C_H0S + d * 256 + hh * 64 + 64]
                                    else:
                                        st = hs[rows, d, hh * 64:hh * 64 + 64]
                                    last = mm(out, st, ec[rows, d, hh, :], start=False, stop=(d == 1))
                        last.then_inc(y_ps, 1)

                fills(pe, L, 2, ada_pair)

                pe.wait_ge(gsq_ready, L * 4 + 1)
                for m in range(4):
                    last = mm(ps[:, 7, 0:T], ones, v[:, m, 0:T], start=(m == 0), stop=(m == 3))
                last.then_inc(ms_ready, 1)

                pe.wait_ge(rstd_ready, L * RSTD + 3)
                for c in range(NCH):
                    for t in range(4):
                        last = tp(ps[:, 5 + c, t * P:t * P + P], u[:, U_RK + t, c * P:c * P + P], ident)
                    last.then_inc(kv_ps, 1)
                pe.wait_ge(kv_ready, L * 3 + 3)
                for s, (c, d) in enumerate(STATE_JOBS):
                    pe.wait_ge(rvt_ready, L * 4 + s + 1)
                    if s >= 2:
                        pe.wait_ge(ret_state, L * 4 + s - 1)
                    for r in range(HR):
                        o = (r % 2) * 64
                        last = mm(ps[o:o + 64, 5 + s % 2, (r // 2) * 64:(r // 2) * 64 + 64],
                                  kvt[:, c, r * 64:r * 64 + 64], vtr[:, r * 64:r * 64 + 64], start=True, stop=True)
                    last.then_inc(rst_ps, 1)
                pe.wait_ge(ret_state, L * 4 + 4)
                pe.wait_ge(ssd_y, L + 1)
                for c in range(NCH):
                    if c:
                        pe.wait_ge(rprob_ready, L * 3 + c)
                    for r in range(HR):
                        rows = slice((r % 2) * 64, (r % 2) * 64 + 64)
                        last = mm(ps[:, 2 + r % 2, (r // 2) * P:(r // 2) * P + P], u[rows, U_RK + r // 2, c * P:c * P + P],
                                  u[rows, U_RQ + r // 2, c * P:c * P + P], start=True, stop=True)
                    last.then_inc(rscore_ps, 1)
                    pe.wait_ge(rprob_ready, L * 3 + c + 1)
                    if c:
                        pe.wait_ge(qr_ready, L * 4 + 2 * c)
                    for r in range(HR):
                        rows = slice((r % 2) * 64, (r % 2) * 64 + 64)
                        m = r // 2
                        out = ps[rows, m, c * P:c * P + P]
                        last = mm(out, kvt[:, c, 256 + r * 64:320 + r * 64], rp[:, r % 2, r // 2, :], start=True, stop=(c == 0))
                        if c:
                            for d in range(2):
                                if (c, d) in ((1, 0), (2, 1)):
                                    st = small[rows, C_H0R + d * 128 + m * 64:C_H0R + d * 128 + m * 64 + 64]
                                else:
                                    st = hr[rows, d, m, :]
                                last = mm(out, st, qr[rows, d, m, :], start=False, stop=(d == 1))
                    last.then_inc(ry_ps, 1)
                pe.wait_ge(ry_taken, L + 1)
                for m in range(2):
                    last = mm(ps[:, 5 + m, 0:T], cc(K_BD), ry[:, m, :], start=True, stop=True)
                last.then_inc(mu_ps, 1)
                pe.wait_ge(centred, L + 1)
                pe.wait_ge(gsq_ready, L * 4 + 2)
                for m in range(2):
                    last = mm(ps[:, 5 + m, 0:T], cc(K_BD), ry2[:, m, :], start=True, stop=True)
                last.then_inc(ms_ready, 1)

                fills(pe, L, 3, ada_pair)

                pe.wait_ge(gsq_ready, L * 4 + 3)
                for m in range(2):
                    last = mm(ps[:, 7, 0:T], ones, nt[:, m, :], start=(m == 0), stop=(m == 1))
                last.then_inc(ms_ready, 1)
                pe.wait_ge(gsq_ready, L * 4 + 4)
                mm(ps[:, 7, 0:T], ones, nt[:, 0, :], start=True, stop=True).then_inc(ms_ready, 1)
                hrow = slice(0, NOPE + ROPE)
                perm = const[hrow, K_PERM:K_PERM + NOPE + ROPE]
                mm(ps[hrow, 6, 0:LAT], perm, u[hrow, U_KR, CTX:T], start=True, stop=True).then_inc(krot_ps, 1)
                pe.wait_ge(qn_ready, L * 2 + 2)
                for h in range(HM):
                    if h >= 2:
                        pe.wait_ge(q_taken, L * HM + h - 1)
                    for k in range(2):
                        c0 = C_UQ + k * 384 + h * 96
                        last = mm(ps[0:96, 2 + h % 2, 0:T], small[:, c0:c0 + 96], u[:, U_MQ + k, :],
                                  start=(k == 0), stop=(k == 1))
                    last.then_inc(q_ps, 1)
                pe.wait_ge(kr_ready, L * 3 + 3)
                pe.wait_ge(q_taken, L * HM + HM)
                for h in range(HM):
                    last = mm(ps[hrow, 5 + h // 2, (h % 2) * LAT:(h % 2) * LAT + LAT], perm, qh[hrow, h, CTX:T],
                              start=True, stop=True)
                    if h % 2:
                        last.then_inc(rot_ps, 1)
                pe.wait_ge(ck_ready, L * 3 + 3)
                for h in range(HM):
                    if h >= 2:
                        pe.wait_ge(k_ready, L * HM + h - 1)
                    c0 = C_UKV + h * 128
                    mm(ps[0:64, h % 2, 0:512], small[:, c0:c0 + 64], ck[:, 0:512], start=True, stop=True)\
                        .then_inc(k_ps, 1)
                wv = small[:, C_UKV:C_UKV + 512].rearrange("p (h n) -> p h n", h=HM)[:, :, 64:128]
                for kt in range(4):
                    if kt >= 2:
                        pe.wait_ge(vm_ready, L * 4 + kt - 1)
                    mm(ps[:, 2 if kt % 2 else 7, 0:256], ck[:, kt * P:kt * P + P], wv, start=True, stop=True)\
                        .then_inc(vm_ps, 1)
                pe.wait_ge(q_ready, L * 2 + 2)
                pe.wait_ge(kh_rope, L + 1)
                pe.wait_ge(k_ready, L * HM + HM)
                pe.wait_ge(vm_ready, L * 4 + 4)

                def keys(c):
                    return (0, 1) if c == 0 else (CTX, 3)

                for i in range(NATT + 3):
                    if i < NATT:
                        c, h = ATT[i]
                        k0, nk = keys(c)
                        if i >= 2:
                            pe.wait_ge(p_exp, L * NATT + i - 1)
                        mm(ps[:, i % 2, 0:nk * P], qh[0:96, h, c * P:c * P + P], kh[0:96, h, k0:k0 + nk * P],
                           start=True, stop=True).then_inc(s_ps, 1)
                    if 0 <= i - 2 < NATT:
                        a = i - 2
                        nk = keys(ATT[a][0])[1]
                        pe.wait_ge(p_ready, L * NATT + a + 1)
                        if a >= 2:
                            pe.wait_ge(pt_ready, L * NATT + a - 1)
                        for kt in range(nk):
                            last = tp(ps[:, 2 + a % 2, kt * P:kt * P + P], pr[:, a % 2, kt * P:kt * P + P], ident)
                        last.then_inc(pt_ps, 1)
                    if 0 <= i - 3:
                        a = i - 3
                        c, h = ATT[a]
                        k0, nk = keys(c)
                        pe.wait_ge(pt_ready, L * NATT + a + 1)
                        o = (h % 2) * 64
                        for kt in range(nk):
                            last = mm(ps[o:o + 64, 5 + h // 2, c * P:c * P + P], vm[:, k0 // P + kt, h * 64:h * 64 + 64],
                                      pt[:, a % 2, kt * P:kt * P + P], start=(kt == 0), stop=(kt == nk - 1))
                        last.then_inc(my_ps, 1)

                pe.wait_ge(mix_ready, L * KD + KD)
                for i in range(N_WOUT):
                    if i >= 2:
                        pe.wait_ge(x_ready, L * 16 + 1 + 2 * (i - 1))
                    wide_block(L, N_WIN + i, i % 2)
                mean_square(L * 16 + KD)
                with pe.Fori(0, N_F1 // 2) as i:
                    pe.wait_ge(h_ready, L * 16 + 2 * KD)
                    for j in range(2):
                        pe.wait_ge(hid_ready, L * N_F1 + i * 2 + (j + 1))
                        wide_block(L, i * 2 + (j + N_WIN + N_WOUT), j)
                with pe.Fori(0, KD // 2) as i:
                    pe.wait_ge(hid_lo_ready, L * KF + KF)
                    for m in range(2):
                        pe.wait_ge(x_ready, L * 16 + i * 2 + (KD + m))
                        for j in range(2):
                            w_ready(L, i * 4 + (2 * m + j + N_WIN + N_WOUT + N_F1))
                            for t in range(KH2):
                                k = j * KH2 + t
                                last = split_mm(ps[:, m, 0:T], wtile(j, t), (hid_hi[:, k, :], hid_lo[:, k, :]), k, KF)
                            last.then_inc(w_used, 1)
            mean_square(16 * DEPTH)

        @block.scalar
        def _(act):
            f = nc.scalar.activation

            def split_hi(L, n, j, width=BLK):
                act.wait_ge(w_used, L * NB + n + 1)
                act.wait_ge(stage_in[j], in_stage(L, n))
                f(whi[:, j, 0:width], stage[:, j, 0:width], ACT.Copy).then_inc(w_hi, 1)

            def in_stage(L, n):
                if isinstance(n, tuple):
                    i, k = n
                    return L * (16 * NB // 2) + i * 16 + 16 * (k // 2 + 1)
                return L * (16 * NB // 2) + 16 * (n // 2 + 1)

            def split_hi_at(L, i, k, j, width=BLK):
                act.wait_ge(w_used, L * NB + i * 2 + (k + 1))
                act.wait_ge(stage_in[j], in_stage(L, (i, k)))
                f(whi[:, j, 0:width], stage[:, j, 0:width], ACT.Copy).then_inc(w_hi, 1)

            def rstd(val, src, width, inv):
                act.wait_ge(ms_ready, val)
                act.wait_ge(rstd_ready, val)
                y = ny[:, 0:width, :]
                f(y, src, ACT.Ln, bias=eps, scale=inv).then_inc(ln_ready, 1)
                act.wait_ge(ln_ready, val)
                f(y, y, ACT.Exp, scale=-0.5).then_inc(y0_ready, 1)

            def squares(L, half):
                for k in range(KD):
                    act.wait_ge(x_ready, L * 16 + (k + 2 if half else 1))
                    f(sq[:, k, :], x[:, k, :], ACT.Square).then_inc(sq_ready, 1)

            def modulate(L, half):
                a, b = (8, 0) if half == 0 else (32, 24)
                act.wait_ge(fact1 if half == 0 else fact2, L * 2 + 2)

                def high(k):
                    act.wait_ge(h_whole, L * 32 + half * 16 + 2 * k + 2)
                    f(h_hi[:, k, :], sq[:, k, :], ACT.Copy).then_inc(h_hi_ready, 1)

                for k in range(KD):
                    act.wait_ge(xn_ready, L * 16 + (half * KD + k + 1))
                    for s, (t0, t1) in enumerate(((0, CTX), (CTX, T))):
                        f(sq[:, k, t0:t1], sq[:, k, t0:t1], ACT.Identity, bias=modl[:, b + k, s:s + 1],
                          scale=modl[:, a + k, s:s + 1]).then_inc(h_whole, 1)
                    if k:
                        high(k - 1)
                high(KD - 1)

            def ffn_tile(L, i, j, width):
                act.wait_ge(w_used, L * NB + i * 2 + (j + N_WIN + N_WOUT + 3))
                act.wait_ge(hid_ready, L * N_F1 + i * 2 + (j + 1))
                f(ny[:, j, :], ps[:, 2 * j, 0:T], ACT.Silu).then_inc(silu_ready, 1)
                split_hi_at(L, i, N_WIN + N_WOUT + j + 2, j, width)
                act.wait_ge(hid_ready, L * N_F1 + i * 2 + (j + 3))
                f(hid_hi[:, bass.ds(i * 2 + j, 1), :], nt[:, j:j + 1, :], ACT.Copy).then_inc(hid_hi_ready, 1)

            def mix_high(L, k, src):
                if k < 6:
                    act.wait_ge(mix_src, L * 6 + k + 1)
                f(h_hi[:, k, :], src, ACT.Copy).then_inc(mix_hi, 1)

            act.wait_ge(const_in, 16)
            f(cond[:], cc(K_COND, 2 * KD).rearrange("p (k s) -> p k s", s=2), ACT.Silu).then_inc(cond_ready, 1)

            with act.Fori(0, DEPTH) as L:
                squares(L, 0)
                split_hi(L, 0, 0, P)
                split_hi(L, 1, 1)
                rstd(L * RSTD + 1, ps[:, 7:8, 0:T], 1, 1.0 / D)
                modulate(L, 0)
                for n in range(N_WIN):
                    act.wait_ge(w_used, L * NB + n + 3)
                    if n:
                        b = 2 * (n % 2)
                        if n <= 3:
                            f(upad[:, 2 * n - 2:2 * n, 2:2 + CTX], ps[:, b:b + 2, 0:CTX], ACT.Copy)
                            last = f(upad[:, 2 * n - 2:2 * n, LATC + 2:LATC + 2 + LAT], ps[:, b:b + 2, CTX:T], ACT.Copy)
                        elif n == 8:
                            f(u[:, U_CKV, :], ps[:, b, 0:T], ACT.Copy)
                            last = f(u[:, U_KR, :], ps[:, b + 1, 0:T], ACT.Copy)
                        else:
                            last = f(u[:, 2 * n - 8:2 * n - 6, :], ps[:, b:b + 2, 0:T], ACT.Copy)
                        last.then_inc(u_ready, 1)
                    split_hi(L, n + 2, n % 2)
                    if n == 0:
                        f(expa[:], sc(C_ALOG, 16), ACT.Exp).then_inc(exps_ready, 1)
                        act.wait_ge(abs_ready, L + 1)
                        f(sps[:], spp[:], ACT.Exp, scale=-1.0).then_inc(exps_ready, 1)
                act.wait_ge(cum_ps, L + 1)
                f(cum[:].rearrange("p d c h -> p (d c h)"), ps[:, 5, 0:48], ACT.Copy).then_inc(cum_ready, 1)
                f(tedt[:].rearrange("p d c h -> p (d c h)"), ps[:, 5, 48:96], ACT.Exp).then_inc(cum_ready, 1)
                f(cd[:].rearrange("p d h -> p (d h)"), ps[:, 5, 96:104], ACT.Exp).then_inc(cum_ready, 1)
                for t in range(6):
                    act.wait_ge(conv_ready, L * 6 + t + 1)
                    f(v[:, t, :], v[:, t, :], ACT.Silu, bias=sc(C_CB + t)).then_inc(v_ready, 1)
                act.wait_ge(u_ready, L * (N_WIN - 1) + N_WIN - 1)
                f(u[:, U_Z:U_Z + 6, :], u[:, U_Z:U_Z + 6, :], ACT.Silu).then_inc(gates_ready, 1)
                for c in range(NCH):
                    act.wait_ge(tr_ps, L * 4 + c + 1)
                    f(xt[:, c, :], ps[:, 5 + c, :], ACT.Copy).then_inc(tr_ready, 1)
                act.wait_ge(tr_ps, L * 4 + 4)
                f(bt[:].rearrange("p c n -> p (c n)"), ps[:, 5, 0:T], ACT.Copy).then_inc(tr_ready, 1)
                for c in range(NCH):
                    for g in range(2):
                        q = 2 * c + g
                        if c:
                            rows = slice(g * 64, g * 64 + 64)
                            act.wait_ge(row_ps, L * 6 + q + 1)
                            act.wait_ge(y_ps, L * 6 + q)
                            f(ec[rows].rearrange("p d h i -> p d (h i)"), ps[rows, 5:7, :], ACT.Exp)\
                                .then_inc(ec_ready, 1)
                        act.wait_ge(seg_ready, L * 6 + q + 1)
                        w = ew[:].rearrange("p d h i -> p (d h i)")
                        f(w, w, ACT.Exp).then_inc(e_ready, 1)
                act.wait_ge(ssd_gated, L * 2 + 2)
                f(v[:, 0:4, 0:T], u[:, U_Z:U_Z + 4, :], ACT.Square).then_inc(gsq_ready, 1)
                rstd(L * RSTD + 2, ps[:, 7:8, 0:T], 1, 1.0 / (HS * 64))
                act.wait_ge(w_used, L * NB + N_WIN + 2)
                for k in range(4):
                    mix_high(L, k, u[:, U_Z + k, :])
                for d in range(2):
                    for r in range(HR):
                        f(rmt[:, d, (r % 2) * 2 + r // 2, :], cc((K_PF, K_PB)[d]), ACT.Exp, scale=lg[:, d * HR + r:d * HR + r + 1])
                    for m in range(2):
                        f(rq[:, d, m, :], cc((K_IP, K_IB)[d]), ACT.Exp, scale=lg[:, 8 + 2 * m + d:9 + 2 * m + d])
                    f(ter[:, d, :], lg[:, d * HR:d * HR + HR], ACT.Exp, scale=cc(K_PC + d, 1))
                f(cdr[:], lg[:, 8:12], ACT.Exp, scale=float(P)).then_inc(rexp_ready, 1)
                for c in range(NCH):
                    act.wait_ge(kv_ps, L * 3 + c + 1)
                    f(kvt[:, c, :], ps[:, 5 + c, :], ACT.Copy).then_inc(kv_ready, 1)
                act.wait_ge(centred, L + 1)
                f(ry2[:], ry[:], ACT.Square).then_inc(gsq_ready, 1)
                rstd(L * RSTD + 3, ps[:, 5:7, 0:T], 2, 1.0)
                for k in range(2):
                    mix_high(L, 4 + k, ry[:, k, :])
                rrow = slice(KR0, KR0 + ROPE)
                act.wait_ge(mix_ready, L * KD + 6)
                f(ck[:, P:2 * P], sc(C_CKV, P), ACT.Copy).then_inc(ck_ready, 1)
                f(kr[rrow, 0:CTX], u[rrow, U_KR, 0:CTX], ACT.Copy).then_inc(kr_ready, 1)
                f(kr[rrow, CTX:2 * P], small[rrow, C_KR:C_KR + P], ACT.Copy).then_inc(kr_ready, 1)
                act.wait_ge(rstd_ready, L * RSTD + 4)
                f(nt[:], u[:, U_MQ:U_MQ + 2, :], ACT.Square).then_inc(gsq_ready, 1)
                rstd(L * RSTD + 4, ps[:, 7:8, 0:T], 1, 1.0 / RANKQ)
                act.wait_ge(rstd_ready, L * RSTD + 5)
                f(nt[:, 0, :], u[:, U_CKV, :], ACT.Square).then_inc(gsq_ready, 1)
                rstd(L * RSTD + 5, ps[:, 7:8, 0:T], 1, 1.0 / RANKKV)
                for h in range(HM):
                    act.wait_ge(q_ps, L * HM + h + 1)
                    f(qh[0:96, h, :], ps[0:96, 2 + h % 2, 0:T], ACT.Copy).then_inc(q_taken, 1)
                for h in range(HM):
                    act.wait_ge(k_ps, L * HM + h + 1)
                    f(kh[0:64, h, :], ps[0:64, h % 2, 0:512], ACT.Copy).then_inc(k_ready, 1)
                for i in range(NATT + 2):
                    if i < NATT:
                        nk = 1 if ATT[i][0] == 0 else 3
                        act.wait_ge(max_ready, L * NATT + i + 1)
                        if i >= 2:
                            act.wait_ge(pt_ps, L * NATT + i - 1)
                        f(pr[:, i % 2, 0:nk * P], ps[:, i % 2, 0:nk * P], ACT.Exp, bias=att[:, 1, i:i + 1], scale=SCALE,
                          accum_out=att[:, 2, i:i + 1]).then_inc(p_exp, 1)
                    if i >= 2:
                        a = i - 2
                        nk = 1 if ATT[a][0] == 0 else 3
                        act.wait_ge(pt_ps, L * NATT + a + 1)
                        if a >= 2:
                            act.wait_ge(my_ps, L * NATT + a - 1)
                        f(pt[:, a % 2, 0:nk * P], ps[:, 2 + a % 2, 0:nk * P], ACT.Copy).then_inc(pt_ready, 1)
                act.wait_ge(my_ps, L * NATT + NATT)
                for k in range(2):
                    mix_high(L, 6 + k, ps[:, 5 + k, 0:T])
                for n in range(N_WIN, N_WIN + N_WOUT):
                    split_hi(L, n + 2, n % 2)
                act.wait_ge(stored, L * 64 + 64)
                squares(L, 1)
                rstd(L * RSTD + 6, ps[:, 7:8, 0:T], 1, 1.0 / D)
                modulate(L, 1)
                with act.Fori(0, N_F1 // 2 - 1) as i:
                    for j in range(2):
                        ffn_tile(L, i, j, BLK)
                for j in range(2):
                    ffn_tile(L, N_F1 // 2 - 1, j, F2BLK)
                with act.Fori(0, N_F2 // 2 - 1) as i:
                    for j in range(2):
                        split_hi_at(L, i, N_WIN + N_WOUT + N_F1 + j + 2, j, F2BLK)
            act.wait_ge(x_ready, 16 * DEPTH + 1)
            for k in range(KD):
                f(sq[:, k, :], x[:, k, :], ACT.Square).then_inc(sq_ready, 1)
            rstd(RSTD * DEPTH + 1, ps[:, 7:8, 0:T], 1, 1.0 / D)

        @block.vector
        def _(dve):
            steps = [0]
            tt, ts, stt = nc.vector.tensor_tensor, nc.vector.tensor_scalar, nc.vector.scalar_tensor_tensor

            def step(L, ins):
                steps[0] += 1
                ins.then_inc(dve_step, 1)
                dve.wait_ge(dve_step, (0 if L is None else L * DVE_STEPS) + steps[0])

            def split_lo(L, n, j, width=BLK):
                if isinstance(n, tuple):
                    dve.wait_ge(w_hi, L * NB + n[0] * 2 + (n[1] + 1))
                else:
                    dve.wait_ge(w_hi, L * NB + (n + 1))
                tt(wlo[:, j, 0:width], stage[:, j, 0:width], whi[:, j, 0:width].bitcast(F32), ALU.subtract)\
                    .then_inc(w_split, 1)

            def ada_mod(pair):
                dve.wait_ge(ada_used, pair * 2 + 4)
                tt(mod[:, bass.ds(pair * 4, 4), :], ps[:, 4, 0:8].rearrange("p (m s) -> p m s", s=2),
                   const[:, bass.ds(pair * 4 + K_BADA, 4)].unsqueeze(2).to_broadcast([P, 4, 2]), ALU.add)\
                    .then_inc(mod_ready, 1)

            def rstd(L, val, src, width, inv):
                n, y, t = nv[:, 0:width, :], ny[:, 0:width, :], nt[:, 0:width, :]
                dve.wait_ge(ln_ready, val)
                ts(n, src, inv, EPS, ALU.mult, ALU.add)
                dve.wait_ge(y0_ready, val)
                step(L, tt(t, y, y, ALU.mult))
                step(L, tt(t, t, n, ALU.mult))
                step(L, ts(t, t, -0.5, 1.5, ALU.mult, ALU.add))
                tt(n, y, t, ALU.mult).then_inc(rstd_ready, 1)
                dve.wait_ge(rstd_ready, val + 1)

            def normed(L, half):
                for k in range(KD):
                    tt(sq[:, k, :], x[:, k, :], nv[:, 0, :], ALU.mult).then_inc(xn_ready, 1)
                for k in range(KD):
                    dve.wait_ge(h_hi_ready, L * 16 + (half * KD + k + 1))
                    tt(h_lo[:, k, :], sq[:, k, :], h_hi[:, k, :].bitcast(F32), ALU.subtract).then_inc(h_ready, 1)

            def mix_low(L, k, src):
                dve.wait_ge(mix_hi, L * KD + k + 1)
                tt(h_lo[:, k, :], src, h_hi[:, k, :].bitcast(F32), ALU.subtract).then_inc(mix_ready, 1)

            def residual(L, bank, m, gate):
                for s, (t0, t1) in enumerate(((0, CTX), (CTX, T))):
                    xm = x[:, m:m + 1, t0:t1] if isinstance(m, int) else x[:, bass.ds(m, 1), t0:t1]
                    gm = modl[:, gate + m, s:s + 1] if isinstance(m, int) else modl[:, bass.ds(m + gate, 1), s]
                    last = stt(xm, ps[:, bank:bank + 1, t0:t1], gm, xm, ALU.mult, ALU.add)
                last.then_inc(x_ready, 1)

            def base(L, k):
                return bass.ds(L * 48 + k, 8)

            nc.vector.memset(upad[:], 0.0).then_inc(dve_step, 1)
            dve.wait_ge(dve_step, 1)
            steps[0] += 1
            first_steps = steps[0]
            dve.wait_ge(const_in, 16)
            dve.wait_ge(x_in, 16)
            dve.sem_inc(x_ready, 1)
            dve.sem_inc(mod_ready, 1)
            dve.sem_inc(rstd_ready, 1)
            dve.sem_inc(w_split, 2)
            dve.sem_inc(hid_ready, 2)
            with dve.Fori(0, 4) as pair:
                ada_mod(pair)

            with dve.Fori(0, DEPTH) as L:
                dve.wait_ge(small_in, L * 16 + 16)
                dve.wait_ge(mod_ready, L * 12 + 5)
                nc.vector.tensor_copy(modl[:, 0:8, :], mod[:, base(L, 0), :]).then_inc(fact1, 1)
                stt(modl[:, 8:16, :], mod[:, base(L, 8), :], 1.0, spread(sc(C_N1, KD), 2, [P, KD]), ALU.add, ALU.mult)\
                    .then_inc(fact1, 1)
                split_lo(L, 0, 0, P)
                split_lo(L, 1, 1)
                rstd(L, L * RSTD + 1, ps[:, 7:8, 0:T], 1, 1.0 / D)
                normed(L, 0)

                ts(spx[:, 48:60], sc(C_LGB, 12), -1.0, None, ALU.mult)
                dve.wait_ge(w_used, L * NB + 3)
                tt(spx[:, 0:48].rearrange("p (c n) -> p c n", c=NCH), ps[:, 0, 0:48].rearrange("p (c n) -> p c n", c=NCH),
                   over(sc(C_DTB, 16), NCH), ALU.add).then_inc(dt_taken, 1)
                dve.wait_ge(dt_taken, L + 1)
                stt(spp[:], spx[:], -1.0, spx[:], ALU.mult, ALU.max).then_inc(abs_ready, 1)
                split_lo(L, 2, 0)
                dve.wait_ge(exps_ready, L * 2 + 2)
                step(L, ts(spq[:], sps[:], 2.0, None, ALU.add))
                step(L, nc.vector.reciprocal(spq[:], spq[:]))
                step(L, tt(sps[:], sps[:], spq[:], ALU.mult))
                step(L, tt(spq[:], sps[:], sps[:], ALU.mult))
                step(L, ts(spp[:], spq[:], 1.0 / 15, None, ALU.mult))
                for odd in (13, 11, 9, 7, 5, 3):
                    step(L, stt(spp[:], spp[:], 1.0 / odd, spq[:], ALU.add, ALU.mult))
                ts(spx[:], spx[:], 0.0, None, ALU.max)
                step(L, stt(spp[:], spp[:], 1.0, sps[:], ALU.add, ALU.mult))
                step(L, stt(dts[:], spp[:], 2.0, spx[:], ALU.mult, ALU.add))
                stt(loga[:].rearrange("p c d h -> p c (d h)"), dts[:, 0:48].rearrange("p (c n) -> p c n", c=NCH), -1.0,
                    over(expa[:], NCH), ALU.mult, ALU.mult).then_inc(loga_ready, 1)
                ts(lg[:], dts[:, 48:60], -1.0, None, ALU.mult).then_inc(loga_ready, 1)
                for n in range(1, N_WIN):
                    split_lo(L, n + 2, n % 2)

                dve.wait_ge(u_ready, L * (N_WIN - 1) + 3)
                for t in range(0, 6, 2):
                    for w in range(CONVW):
                        for a in (t, t + 1):
                            xin, wc = upad[:, a, w:w + CONVT], sc(C_CW + w * 6 + a)
                            if w == 0:
                                ins = ts(v[:, a, :], xin, wc, None, ALU.mult)
                            else:
                                ins = stt(v[:, a, :], xin, wc, v[:, a, :], ALU.mult, ALU.add)
                            if w == CONVW - 1:
                                ins.then_inc(conv_ready, 1)
                            elif a == t + 1:
                                step(L, ins)

                fills_mod = ada_mod
                fills(dve, L, 0, fills_mod)
                dve.wait_ge(cum_ready, L * 3 + 3)
                for d in range(2):
                    tt(tedt[:, d], tedt[:, d], dts[:, 0:48].rearrange("p (c d h) -> p d c h", c=NCH, d=2)[:, d],
                       ALU.mult).then_inc(tedt_ready, 1)
                for s, (c, d) in enumerate(STATE_JOBS):
                    bank = ps[:, 6 + s % 2, 0:256]
                    dve.wait_ge(st_ps, L * 4 + s + 1)
                    if s < 2:
                        nc.vector.tensor_copy(sout[:, d, :], bank).then_inc(ssd_state, 1)
                    else:
                        h4 = "p (h n) -> p h n"
                        step(L, tt(hs[:, d, :].rearrange(h4, h=HSG), sc(C_H0S + d * 256, 256).rearrange(h4, h=HSG),
                                   spread(cd[:, d, :], 64, [P, HSG]), ALU.mult))
                        tt(hs[:, d, :], hs[:, d, :], bank, ALU.add).then_inc(ssd_state, 1)

                fills(dve, L, 1, fills_mod)
                for c in range(NCH):
                    for g in range(2):
                        q = 2 * c + g
                        dve.wait_ge(score_ps, L * 6 + q + 1)
                        for d in range(2):
                            tt(stm[:, d, g, :], ps[:, 7, 0:P], tri[d], ALU.mult).then_inc(stm_ready, 1)
                        dve.wait_ge(row_ps, L * 6 + q + 1)
                        if q:
                            dve.wait_ge(y_ps, L * 6 + q)
                        if c:
                            dve.wait_ge(ec_ready, L * 4 + q - 1)
                        for d in range(2):
                            for hh in range(HSG):
                                h = g * HSG + hh
                                last = ts(ew[:, d, hh, :], ps[:, 5 + d, hh * P:hh * P + P], cum[:, d, c, h:h + 1], 0.0,
                                          ALU.subtract, ALU.min)
                        last.then_inc(seg_ready, 1)
                        if c:
                            rows = slice(g * 64, g * 64 + 64)
                            w = ec[rows].rearrange("p d h i -> p (d h) i")
                            tt(w, w, over(v[rows, 5, CS[c]:CS[c] + P], 2 * HSG), ALU.mult).then_inc(qsc_ready, 1)
                        dve.wait_ge(e_ready, L * 6 + q + 1)
                        dve.wait_ge(stm_ready, L * 12 + 2 * q + 2)
                        for d in range(2):
                            tt(ew[:, d], ew[:, d], over(stm[:, d, g, :], HSG), ALU.mult).then_inc(prob_ready, 1)
                dve.wait_ge(y_ps, L * 6 + 6)
                for m in range(4):
                    for c0, t0, t1 in ((0, 0, CTX), (LATC, CTX, T)):
                        vin = v[:, m, c0:c0 + t1 - t0]
                        last = stt(vin, vin, sc(C_DSK + m), ps[:, m, t0:t1], ALU.mult, ALU.add)
                last.then_inc(ssd_y, 1)
                dve.wait_ge(ssd_y, L + 1)
                dve.wait_ge(gates_ready, L + 1)
                for c0, t0, t1 in ((0, 0, CTX), (LATC, CTX, T)):
                    z = u[:, U_Z:U_Z + 4, t0:t1]
                    tt(z, z, v[:, 0:4, c0:c0 + t1 - t0], ALU.mult).then_inc(ssd_gated, 1)
                fills(dve, L, 2, fills_mod)
                rstd(L, L * RSTD + 2, ps[:, 7:8, 0:T], 1, 1.0 / (HS * 64))
                for m in range(4):
                    z = u[:, U_Z + m, :]
                    stt(z, z, sc(C_SN + m), nv[:, 0, :], ALU.mult, ALU.mult).then_inc(mix_src, 1)
                for m in range(4):
                    mix_low(L, m, u[:, U_Z + m, :])

                dve.wait_ge(rexp_ready, L + 1)
                for d in range(2):
                    last = stt(rmt[:, d], rmt[:, d], 0.125, over(tri[d], HR), ALU.mult, ALU.mult)
                step(L, last)
                tt(rm[:].rearrange("p o m i -> p (o m) i"), rmt[:, 0], rmt[:, 1], ALU.add).then_inc(rmat_ready, 1)
                ts(ter[:], ter[:], 0.125, None, ALU.mult).then_inc(rmat_ready, 1)
                for s, (c, d) in enumerate(STATE_JOBS):
                    dve.wait_ge(rst_ps, L * 4 + s + 1)
                    bank = ps[:, 5 + s % 2, 0:128].rearrange("p (m n) -> p m n", m=2)
                    if s < 2:
                        last = nc.vector.tensor_copy(rout[:, d], bank)
                    else:
                        for m in range(2):
                            last = stt(hr[:, d, m, :], sc(C_H0R + d * 128 + m * 64, 64), cdr[:, 2 * m + d:2 * m + d + 1],
                                       bank[:, m, :], ALU.mult, ALU.add)
                    last.then_inc(ret_state, 1)
                dve.wait_ge(rmat_ready, L * 2 + 2)
                for c in range(NCH):
                    dve.wait_ge(rscore_ps, L * 3 + c + 1)
                    if c:
                        dve.wait_ge(ry_ps, L * 3 + c)
                    tt(rp[:], ps[:, 2:4, 0:256].rearrange("p o (m i) -> p o m i", m=2), rm[:], ALU.mult)\
                        .then_inc(rprob_ready, 1)
                dve.wait_ge(ry_ps, L * 3 + 3)
                nc.vector.tensor_copy(ry[:], ps[:, 0:2, 0:T]).then_inc(ry_taken, 1)
                dve.wait_ge(mu_ps, L + 1)
                tt(ry[:], ry[:], ps[:, 5:7, 0:T], ALU.subtract).then_inc(centred, 1)
                rstd(L, L * RSTD + 3, ps[:, 5:7, 0:T], 2, 1.0)
                for m in range(2):
                    step(L, stt(ry[:, m, :], ry[:, m, :], sc(C_GN + m), nv[:, m, :], ALU.mult, ALU.mult))
                    tt(ry[:, m, :], ry[:, m, :], u[:, U_G + m, :], ALU.mult).then_inc(mix_src, 1)
                for m in range(2):
                    mix_low(L, 4 + m, ry[:, m, :])
                fills(dve, L, 3, fills_mod)

                rstd(L, L * RSTD + 4, ps[:, 7:8, 0:T], 1, 1.0 / RANKQ)
                for m in range(2):
                    q = u[:, U_MQ + m, :]
                    stt(q, q, sc(C_QN + m), nv[:, 0, :], ALU.mult, ALU.mult).then_inc(qn_ready, 1)
                dve.wait_ge(qn_ready, L * 2 + 2)
                rstd(L, L * RSTD + 5, ps[:, 7:8, 0:T], 1, 1.0 / RANKKV)
                for k0, t0, t1 in ((0, 0, CTX), (2 * P, CTX, T)):
                    stt(ck[:, k0:k0 + t1 - t0], u[:, U_CKV, t0:t1], sc(C_KN), nv[:, 0, t0:t1], ALU.mult, ALU.mult)\
                        .then_inc(ck_ready, 1)
                rrow = slice(KR0, KR0 + ROPE)
                cos, sin = const[rrow, K_COS:K_COS + LAT], const[rrow, K_SIN:K_SIN + LAT]
                dve.wait_ge(krot_ps, L + 1)
                tt(rt[rrow, 0, :], ps[rrow, 6, 0:LAT], sin, ALU.mult)
                step(L, tt(kr[rrow, 256:512], u[rrow, U_KR, CTX:T], cos, ALU.mult))
                tt(kr[rrow, 256:512], kr[rrow, 256:512], rt[rrow, 0, :], ALU.add).then_inc(kr_ready, 1)
                dve.wait_ge(kr_ready, L * 3 + 3)
                nc.vector.tensor_copy(kh[rrow, :, :], over(kr[rrow, :], HM)).then_inc(kh_rope, 1)
                for hp in range(2):
                    dve.wait_ge(rot_ps, L * 2 + hp + 1)
                    if hp:
                        dve.wait_ge(q_ready, L * 2 + hp)
                    q = qh[rrow, 2 * hp:2 * hp + 2, CTX:T]
                    tt(rt[rrow], ps[rrow, 5 + hp, :].rearrange("p (h t) -> p h t", h=2), over(sin, 2), ALU.mult)
                    step(L, tt(q, q, over(cos, 2), ALU.mult))
                    tt(q, q, rt[rrow], ALU.add).then_inc(q_ready, 1)
                for kt in range(4):
                    dve.wait_ge(vm_ps, L * 4 + kt + 1)
                    nc.vector.tensor_copy(vm[:, kt, :], ps[:, 2 if kt % 2 else 7, 0:256]).then_inc(vm_ready, 1)
                for i in range(NATT + 1):
                    if i < NATT:
                        nk = 1 if ATT[i][0] == 0 else 3
                        dve.wait_ge(s_ps, L * NATT + i + 1)
                        step(L, nc.vector.reduce_max(att[:, 0, i:i + 1], ps[:, i % 2, 0:nk * P], AX_X))
                        ts(att[:, 1, i:i + 1], att[:, 0, i:i + 1], -SCALE, None, ALU.mult).then_inc(max_ready, 1)
                    if i >= 1:
                        a = i - 1
                        nk = 1 if ATT[a][0] == 0 else 3
                        dve.wait_ge(p_exp, L * NATT + a + 1)
                        step(L, nc.vector.reciprocal(att[:, 3, a:a + 1], att[:, 2, a:a + 1]))
                        w = pr[:, a % 2, 0:nk * P]
                        ts(w, w, att[:, 3, a:a + 1], None, ALU.mult).then_inc(p_ready, 1)
                for k in range(2):
                    mix_low(L, 6 + k, ps[:, 5 + k, 0:T])

                dve.wait_ge(mod_ready, L * 8 + 17)
                nc.vector.tensor_copy(modl[:, 16:24, :], mod[:, base(L, 16), :])
                nc.vector.tensor_copy(modl[:, 24:32, :], mod[:, base(L, 24), :]).then_inc(fact2, 1)
                nc.vector.tensor_copy(modl[:, 40:48, :], mod[:, base(L, 40), :])
                stt(modl[:, 32:40, :], mod[:, base(L, 32), :], 1.0, spread(sc(C_N2, KD), 2, [P, KD]), ALU.add,
                    ALU.mult).then_inc(fact2, 1)
                dve.wait_ge(fact2, L * 2 + 2)
                for i in range(N_WOUT):
                    n = N_WIN + i
                    dve.wait_ge(w_used, L * NB + n + 3)
                    for s in range(2):
                        residual(L, 2 * (i % 2) + s, 2 * i + s, 16)
                    split_lo(L, n + 2, n % 2)
                rstd(L, L * RSTD + 6, ps[:, 7:8, 0:T], 1, 1.0 / D)
                normed(L, 1)

                def ffn_tile(i, j, width):
                    dve.wait_ge(silu_ready, L * N_F1 + i * 2 + (j + 1))
                    tt(nt[:, j, :], ny[:, j, :], ps[:, 2 * j + 1, 0:T], ALU.mult).then_inc(hid_ready, 1)
                    split_lo(L, (i, N_WIN + N_WOUT + j + 2), j, width)
                    dve.wait_ge(hid_hi_ready, L * N_F1 + i * 2 + (j + 1))
                    hk = bass.ds(i * 2 + j, 1)
                    tt(hid_lo[:, hk, :], nt[:, j:j + 1, :], hid_hi[:, hk, :].bitcast(F32), ALU.subtract)\
                        .then_inc(hid_lo_ready, 1)

                with dve.Fori(0, N_F1 // 2 - 1) as i:
                    for j in range(2):
                        ffn_tile(i, j, BLK)
                for j in range(2):
                    ffn_tile(N_F1 // 2 - 1, j, F2BLK)

                def ffn_out(i, m, more):
                    for j in range(2):
                        k = 2 * m + j + N_WIN + N_WOUT + N_F1
                        if m == 0 or more:
                            dve.wait_ge(w_hi, L * NB + i * 4 + (k + 3))
                            tt(wlo[:, j, 0:F2BLK], stage[:, j, 0:F2BLK], whi[:, j, 0:F2BLK].bitcast(F32),
                               ALU.subtract).then_inc(w_split, 1)
                    dve.wait_ge(w_used, L * NB + i * 4 + (2 * m + 1 + N_WIN + N_WOUT + N_F1 + 3))
                    residual(L, m, i * 2 + m, 40)

                with dve.Fori(0, KD // 2 - 1) as i:
                    for m in range(2):
                        ffn_out(i, m, True)
                for m in range(2):
                    ffn_out(KD // 2 - 1, m, False)
            assert steps[0] == DVE_STEPS + first_steps, steps[0] - first_steps
            steps[0] = first_steps + DVE_STEPS * DEPTH
            rstd(None, RSTD * DEPTH + 1, ps[:, 7:8, 0:T], 1, 1.0 / D)
            for k in range(KD):
                stt(sq[:, k, :], x[:, k, :], cc(K_FN + k, 1), nv[:, 0, :], ALU.mult, ALU.mult).then_inc(y_ready, 1)

        @block.gpsimd
        def _(pool):
            g = nc.gpsimd
            dtv = dts[:, 0:48].rearrange("p (c d h) -> p c d h", c=NCH, d=2)
            with pool.Fori(0, DEPTH) as L:
                pool.wait_ge(tedt_ready, L * 2 + 2)
                pool.wait_ge(tr_ready, L * 4 + 4)
                h8 = "p (h n) -> p h n"
                for s, (c, d) in enumerate(STATE_JOBS):
                    if s:
                        pool.wait_ge(st_ps, L * 4 + s)
                    g.tensor_tensor(vte[:].rearrange(h8, h=HS), xt[:, c, :].rearrange(h8, h=HS),
                                    spread(tedt[:, d, c, :], 64, [P, HS]), ALU.mult).then_inc(vte_ready, 1)
                for c in range(NCH):
                    if c:
                        pool.wait_ge(y_ps, L * 6 + 2 * c)
                    for d in range(2):
                        g.tensor_tensor(vd[:, d].rearrange(h8, h=HS), xt[:, c, :].rearrange(h8, h=HS),
                                        spread(dtv[:, c, d, :], 64, [P, HS]), ALU.mult).then_inc(vd_ready, 1)
                pool.wait_ge(rmat_ready, L * 2 + 2)
                pool.wait_ge(kv_ready, L * 3 + 3)
                for s, (c, d) in enumerate(STATE_JOBS):
                    if s:
                        pool.wait_ge(rst_ps, L * 4 + s)
                    g.tensor_tensor(vtr[:].rearrange(h8, h=HR), kvt[:, c, 256:512].rearrange(h8, h=HR),
                                    spread(ter[:, d, :], 64, [P, HR]), ALU.mult).then_inc(rvt_ready, 1)
                for c in range(1, NCH):
                    if c > 1:
                        pool.wait_ge(ry_ps, L * 3 + c)
                    for d in range(2):
                        g.tensor_tensor(qr[:, d], u[:, U_RQ:U_RQ + 2, c * P:c * P + P], rq[:, d], ALU.mult)\
                            .then_inc(qr_ready, 1)


def constants(b_ada, final_w, conds):
    a = np.zeros((P, CONSTW), np.float32)
    t = np.arange(P)
    a[:, K_ID:K_ID + P] = np.eye(P)
    a[:, K_U:K_U + P] = t[:, None] <= t
    a[:, K_L:K_L + P] = t[:, None] >= t
    a[:, K_SU:K_SU + P] = t[:, None] < t
    a[:, K_SL:K_SL + P] = t[:, None] > t
    a[:, K_BD:K_BD + P] = (t[:, None] // 64 == t // 64) / 64.0
    a[:, K_ONE:K_ONE + P] = 1.0
    a[:, K_PF:K_PF + P] = np.maximum(t - t[:, None], 0)
    a[:, K_PB:K_PB + P] = np.maximum(t[:, None] - t, 0)
    a[:, K_IP:K_IP + P] = t + 1
    a[:, K_IB:K_IB + P] = P - t
    a[:, K_PC], a[:, K_PC + 1] = P - 1 - t, t
    a[:, K_EPS] = EPS
    half = ROPE // 2
    inv = np.float32(10000.0) ** (-np.arange(0, half, 2, dtype=np.float32) / np.float32(half))
    pos = np.arange(LAT)
    ar = (pos // 64).astype(np.float32)[:, None] * inv
    ac = (pos % 64).astype(np.float32)[:, None] * inv
    ang = np.concatenate([ar, ar, ac, ac], 1).T
    a[KR0:KR0 + ROPE, K_COS:K_COS + LAT] = np.cos(ang)
    a[KR0:KR0 + ROPE, K_SIN:K_SIN + LAT] = np.sin(ang)
    for m in range(ROPE):
        if m % half < half // 2:
            a[KR0 + m + half // 2, K_PERM + KR0 + m] = -1.0
        else:
            a[KR0 + m - half // 2, K_PERM + KR0 + m] = 1.0
    a[:, K_BADA:K_BADA + DEPTH * 48] = b_ada
    a[:, K_FN:K_FN + KD] = final_w
    a[:, K_COND:K_COND + 2 * KD] = conds
    return a


OUTS = [(P, KD, T), (DEPTH, P, 512), (DEPTH, P, 256), (DEPTH, P, CTX), (DEPTH, ROPE, CTX)]


def kernel(x_prompt, x_sample, c, state_ssd, state_ret, cache_mla_ckv, cache_mla_krope, c_ctx, w_ada, b_ada, norm1_w,
           w_in, ssd_conv_w, ssd_conv_b, ssd_dt_bias, ssd_A_log, ssd_D, ssd_norm_w, ret_decay_logit, ret_gn_w,
           mla_q_norm_w, mla_w_uq, mla_kv_norm_w, mla_w_ukv, w_out, norm2_w, ffn_w1, ffn_w2, final_norm_w):
    import concourse.bacc as _bacc
    from concourse.bass_utils import run_bass_kernel_spmd as _run

    n = DEPTH
    cat = np.concatenate
    arr = np.asarray

    def tiles(a):
        a = arr(a)
        return np.moveaxis(a.reshape(*a.shape[:-1], -1, P), -1, -2)

    def blocks(a, width):
        a = arr(a)
        k, m = a.shape[1] // P, a.shape[2] // width
        return a.reshape(n, k, P, m, width).transpose(0, 3, 2, 1, 4).reshape(n, m, P, k * width)

    def everywhere(a):
        a = arr(a).reshape(n, 1, -1)
        return np.broadcast_to(a, (n, P, a.shape[2]))

    def by_rows(a):
        a = np.moveaxis(arr(a).reshape(n, -1, arr(a).shape[-1] // 2, 2), 1, 2)
        a = np.moveaxis(a, 3, 1).reshape(n, 2, -1)
        return np.repeat(a, 64, axis=1)

    xt = cat([arr(x_prompt)[0], arr(x_sample)[0]]).T.reshape(KD, P, T).transpose(1, 0, 2)
    w_in = arr(w_in)
    starts = (512, 768, 1024, 1296, 1552, 1808, 2320, None, 0, 256, 2064)
    cols = [w_in[:, :, s:s + 256] if s is not None else
            cat([w_in[:, :, 2576:2704], w_in[:, :, 2640:2736], np.zeros((n, D, 32), np.float32)], axis=2)
            for s in starts]
    win = blocks(cat(cols, axis=2), 256).reshape(n * (N_WIN - 1), P, BLK)
    wdt = blocks(w_in[:, :, 1280:1296], 16).reshape(n, P, P)
    wout = blocks(w_out, 256).reshape(n * N_WOUT, P, BLK)
    f1 = arr(ffn_w1).reshape(n, D, 2, KF, P).transpose(0, 1, 3, 2, 4).reshape(n, D, 2 * DFF)
    wf1 = blocks(f1, 256).reshape(n * N_F1, P, BLK)
    wf2 = arr(ffn_w2).reshape(n, 2, KH2, P, KD, P).transpose(0, 4, 1, 3, 2, 5).reshape(n * N_F2, P, F2BLK)
    wada = blocks(w_ada, 256).reshape(n * 24, P, BLK)

    kr = np.zeros((n, P, P), np.float32)
    kr[:, KR0:KR0 + ROPE] = arr(cache_mla_krope)[0].transpose(0, 2, 1)
    h0s = arr(state_ssd)[0].reshape(n, 2, 2, HSG, 64, 64).transpose(0, 2, 4, 1, 3, 5).reshape(n, P, 512)
    h0r = arr(state_ret)[0].reshape(n, 2, 2, 2, 64, 64).transpose(0, 3, 4, 1, 2, 5).reshape(n, P, 256)
    small = cat([
        tiles(norm1_w), tiles(norm2_w),
        tiles(ssd_conv_w).transpose(0, 2, 1, 3).reshape(n, P, -1), tiles(ssd_conv_b), tiles(ssd_norm_w),
        tiles(ret_gn_w), tiles(mla_q_norm_w), tiles(mla_kv_norm_w), by_rows(ssd_D),
        everywhere(ssd_dt_bias), everywhere(ssd_A_log), everywhere(ret_decay_logit), by_rows(ret_decay_logit),
        h0s, h0r, arr(cache_mla_ckv)[0].transpose(0, 2, 1), kr,
        arr(mla_w_uq).reshape(n, 2, P, 384).transpose(0, 2, 1, 3).reshape(n, P, 768), arr(mla_w_ukv)], axis=2)
    assert small.shape[2] == SMALLW
    conds = np.stack([tiles(arr(c_ctx)), tiles(arr(c)[0])], axis=-1).reshape(P, 2 * KD)
    const = constants(tiles(b_ada).transpose(1, 0, 2).reshape(P, n * 48), tiles(final_norm_w), conds)

    nc = _bacc.Bacc("TRN2", target_bir_lowering=False, num_devices=1)
    arrays, args = {}, []
    for name, a in dict(x=xt, const=const, small=small, win=win, wdt=wdt, wout=wout, wf1=wf1, wf2=wf2,
                        wada=wada).items():
        a = np.ascontiguousarray(a)
        arrays[f"{name}_dram"] = a
        args.append(nc.dram_tensor(f"{name}_dram", a.shape, mybir.dt.from_np(a.dtype), kind="ExternalInput").ap())
    for i, shape in enumerate(OUTS):
        args.append(nc.dram_tensor(f"out_{i}_dram", shape, F32, kind="ExternalOutput").ap())
    program(nc, *args)
    r = _run(nc, [arrays], core_ids=[0]).results[0]
    y, ss, sr, ckv, krope = (r[f"out_{i}_dram"] for i in range(len(OUTS)))
    y = y.transpose(2, 1, 0).reshape(T, D)
    ss = ss.reshape(n, 2, 64, 2, HSG, 64).transpose(0, 3, 1, 4, 2, 5).reshape(1, n, 2, HS, 64, 64)
    sr = sr.reshape(n, 2, 64, 2, 2, 64).transpose(0, 3, 4, 1, 2, 5).reshape(1, n, 2, HR, 64, 64)
    return (np.ascontiguousarray(y[:CTX])[None], np.ascontiguousarray(y[CTX:])[None], np.ascontiguousarray(ss),
            np.ascontiguousarray(sr), np.ascontiguousarray(ckv.transpose(0, 2, 1))[None],
            np.ascontiguousarray(krope.transpose(0, 2, 1))[None])
```

```python
from contextlib import ExitStack

import numpy as np

import concourse.bass as bass
from concourse import mybir

F32 = mybir.dt.float32
F32R = mybir.dt.float32r
ALU = mybir.AluOpType
ACT = mybir.ActivationFunctionType
AX_X = mybir.AxisListType.X

P = 128
D = 1024
KD = D // P
DEPTH = 2
CTX, LAT = 128, 256
T = CTX + LAT
NCH = T // P
EPS = 1e-6
HS, HSG, NS = 8, 4, 64
HR, HM = 4, 4
RANKQ, RANKKV, ROPE, NOPE = 256, 128, 32, 64
DFF = 2816
KF = DFF // P
KH2 = KF // 2
SCALE = float(NOPE + ROPE) ** -0.5
CONVW = 5
PADT = T + 8
CONVT = T + 4
CS = (0, 132, 260)
LATC = CS[1]

BLK = KD * 2 * P
N_WIN, N_WOUT, N_F1, N_F2 = 12, 4, KF, 2 * KD
KW2 = KD // 2
F2BLK = KH2 * P
NB = N_WIN + N_WOUT + N_F1 + N_F2
PART_TILES = 8
TURNS = 5
CW = 32
ADA_BESIDE = {1: (0, 1), 2: (2, 3), 3: (4, 5), 4: (6, 7)}


def ada_order():
    turns = [(0, 1)]
    for layer in range(DEPTH):
        first = 6 * layer
        turns += [(first + 2,), (first + 3, first + 4)] + [(p,) for p in range(first + 5, min(first + 8, 6 * DEPTH))]
    return [(p, k) for turn in turns for k in range(KD) for p in turn]


assert DEPTH == 2

def columns(*widths):
    return np.concatenate([[0], np.cumsum(widths)]).tolist()


(C_N1, C_N2, C_CW, C_CB, C_SN, C_GN, C_QN, C_KN, C_DSK, C_DTB, C_ALOG, C_LGB, C_LGC, C_H0S, C_H0R, C_CKV, C_KR,
 C_UQ, C_UKV, SMALLW) = columns(KD, KD, CONVW * 6, 6, 4, 2, 2, 1, 4, 16, 16, 8, 4, 512, 256, P, P, 768, 512)
(K_ID, K_U, K_L, K_SU, K_SL, K_BD, K_ONE, K_PF, K_PB, K_IP, K_IB, K_COS, K_SIN, K_PERM, K_PC, K_EPS, K_BADA, K_FN,
 K_COND, CONSTW) = columns(*[P] * 11, LAT, LAT, NOPE + ROPE, 2, 1, DEPTH * 48, KD, 2 * KD)

U_RQ, U_RK, U_RV, U_MQ, U_CKV, U_KR, U_Z, U_G = 0, 2, 4, 6, 8, 9, 10, 14
KR0 = NOPE

DVE_STEPS = 68
RSTD = 6
ATT = [(c, h) for c in range(NCH) for h in range(HM)]
NATT = len(ATT)


def program(nc, x_d, const_d, small_d, win_d, wdt_d, wout_d, wf1_d, wf2_d, wada_d, y_d, sssd_d, sret_d, ckv_d, kr_d):
    with ExitStack() as ctx:
        def sb(name, shape, dt=F32, stack=ctx):
            return stack.enter_context(nc.sbuf_tensor(name, shape, dt))

        def sem(name):
            return ctx.enter_context(nc.semaphore(name))

        stage_in0 = sem("stage_in0")
        stage_in1 = sem("stage_in1")
        ada_in0 = sem("ada_in0")
        ada_in1 = sem("ada_in1")
        ada_in2 = sem("ada_in2")
        ada_in3 = sem("ada_in3")
        const_in = sem("const_in")
        x_in = sem("x_in")
        small_in = sem("small_in")
        w_hi = sem("w_hi")
        w_split = sem("w_split")
        w_used = sem("w_used")
        ada_used = sem("ada_used")
        ada_out = sem("ada_out")
        ada_tr = sem("ada_tr")
        mod_ready = sem("mod_ready")
        zeroed = sem("zeroed")
        cond_ready = sem("cond_ready")
        fact1 = sem("fact1")
        gate2_ready = sem("gate2_ready")
        gate1_ready = sem("gate1_ready")
        hs_decayed = sem("hs_decayed")
        fact2 = sem("fact2")
        sq_ready = sem("sq_ready")
        sq_used = sem("sq_used")
        gsq_ready = sem("gsq_ready")
        ms_ready = sem("ms_ready")
        ln_ready = sem("ln_ready")
        y0_ready = sem("y0_ready")
        rstd_ready = sem("rstd_ready")
        xn_ready = sem("xn_ready")
        h_whole = sem("h_whole")
        h_hi_ready = sem("h_hi_ready")
        h_ready = sem("h_ready")
        u_ready = sem("u_ready")
        conv_ready = sem("conv_ready")
        v_ready = sem("v_ready")
        dt_taken = sem("dt_taken")
        dt_tr = sem("dt_tr")
        abs_ready = sem("abs_ready")
        exps_ready = sem("exps_ready")
        loga_ready = sem("loga_ready")
        cum_ps = sem("cum_ps")
        cum_ready = sem("cum_ready")
        tedt_ready = sem("tedt_ready")
        tr_ps = sem("tr_ps")
        tr_ready = sem("tr_ready")
        vte_ready = sem("vte_ready")
        st_ps = sem("st_ps")
        ssd_state = sem("ssd_state")
        score_ps = sem("score_ps")
        stm_ready = sem("stm_ready")
        row_ps = sem("row_ps")
        ec_ready = sem("ec_ready")
        qsc_ready = sem("qsc_ready")
        seg_ready = sem("seg_ready")
        e_ready = sem("e_ready")
        prob_ready = sem("prob_ready")
        vd_ready = sem("vd_ready")
        y_ps = sem("y_ps")
        ssd_y = sem("ssd_y")
        gates_ready = sem("gates_ready")
        ssd_gated = sem("ssd_gated")
        rexp_ready = sem("rexp_ready")
        rmat_ready = sem("rmat_ready")
        kv_ps = sem("kv_ps")
        kv_ready = sem("kv_ready")
        rvt_ready = sem("rvt_ready")
        rst_ps = sem("rst_ps")
        ret_state = sem("ret_state")
        rscore_ps = sem("rscore_ps")
        rprob_ready = sem("rprob_ready")
        qr_ready = sem("qr_ready")
        ry_ps = sem("ry_ps")
        ry_taken = sem("ry_taken")
        mu_ps = sem("mu_ps")
        centred = sem("centred")
        qn_ready = sem("qn_ready")
        ck_ready = sem("ck_ready")
        krot_ps = sem("krot_ps")
        kr_ready = sem("kr_ready")
        kh_rope = sem("kh_rope")
        q_ps = sem("q_ps")
        q_taken = sem("q_taken")
        rot_ps = sem("rot_ps")
        q_ready = sem("q_ready")
        k_ps = sem("k_ps")
        k_ready = sem("k_ready")
        vm_ps = sem("vm_ps")
        vm_ready = sem("vm_ready")
        s_ps = sem("s_ps")
        max_ready = sem("max_ready")
        p_exp = sem("p_exp")
        p_ready = sem("p_ready")
        pt_ps = sem("pt_ps")
        pt_ready = sem("pt_ready")
        my_ps = sem("my_ps")
        mix_src = sem("mix_src")
        mix_hi = sem("mix_hi")
        mix_ready = sem("mix_ready")
        wo_ps = sem("wo_ps")
        x_ready = sem("x_ready")
        silu_ready = sem("silu_ready")
        hid_ready = sem("hid_ready")
        hid_hi_ready = sem("hid_hi_ready")
        hid_lo_ready = sem("hid_lo_ready")
        y_ready = sem("y_ready")
        dve_step = sem("dve_step")
        stored = sem("stored")
        stage_in, ada_in = (stage_in0, stage_in1), (ada_in0, ada_in1, ada_in2, ada_in3)

        x = sb("x", [P, KD, T])
        h_hi, h_lo = sb("h_hi", [P, KD, T], F32R), sb("h_lo", [P, KD, T], F32R)
        stage = sb("stage", [P, 2, BLK])
        whi, wlo = sb("whi", [P, 2, BLK], F32R), sb("wlo", [P, 2, BLK], F32R)
        dthi, dtlo = sb("dthi", [P, P], F32R), sb("dtlo", [P, P], F32R)
        adas = sb("adas", [P, 4, BLK // 2])
        small = sb("small", [P, SMALLW])
        const = sb("const", [P, CONSTW])
        cond = sb("cond", [P, KD, CW])
        adac = sb("adac", [P, 512])
        mod = sb("mod", [P, DEPTH * 48, 2])
        modl = sb("modl", [P, 48, 2])
        nv, ny, nt = (sb(n, [P, 2, T]) for n in ("nv", "ny", "nt"))
        upad = sb("upad", [P, 6, PADT])
        ps = ctx.enter_context(nc.psum_tensor("ps", [P, 8, 512], F32))

        with ExitStack() as region:
            hid_hi, hid_lo = (sb(n, [P, KF, T], F32R, region) for n in ("hid_hi", "hid_lo"))
        with ExitStack() as region:
            sq = sb("sq", [P, KD, T], F32, region)
            adaf = sb("adaf", [P, 3, 4, D], F32, region)
        with ExitStack() as region:
            u = sb("u", [P, 16, T], F32, region)
            bt = sb("bt", [P, NCH, P], F32, region)
            dts = sb("dts", [P, 60], F32, region)
            spx, spp, sps, spq = (sb(n, [P, 60], F32, region) for n in ("spx", "spp", "sps", "spq"))
            loga = sb("loga", [P, NCH, 2, HS], F32, region)
            expa = sb("expa", [P, 16], F32, region)
            lg = sb("lg", [P, 12], F32, region)
            cum = sb("cum", [P, 2, NCH, HS], F32, region)
            tedt = sb("tedt", [P, 2, NCH, HS], F32, region)
            cd = sb("cd", [P, 2, HSG], F32, region)
            hs = sb("hs", [P, 2, 256], F32, region)
            hr = sb("hr", [P, 2, 2, 64], F32, region)
            sout = sb("sout", [P, 2, 256], F32, region)
            rout = sb("rout", [P, 2, 2, 64], F32, region)
            att = sb("att", [P, 4, NATT], F32, region)
            ter = sb("ter", [P, 2, HR], F32, region)
            cdr = sb("cdr", [P, 4], F32, region)
            with ExitStack() as part:
                v = sb("v", [P, 6, CONVT], F32, part)
                xt = sb("xt", [P, NCH, 512], F32, part)
                vd = sb("vd", [P, 2, 512], F32, part)
                ew = sb("ew", [P, 2, HSG, P], F32, part)
                stm = sb("stm", [P, 2, 2, P], F32, part)
                with ExitStack() as edge:
                    ec = sb("ec", [P, 2, HSG, P], F32, edge)
                gsq = sb("gsq", [P, 4, T], F32, part)
                vte = [a[:, d].rearrange("p h i -> p (h i)") for a in (ew,) for d in range(2)] + [vd[:, d] for d in range(2)]
            lat = slice(LATC + 2, LATC + 2 + LAT)
            rmt = [upad[:, 2 * d:2 * d + 2, lat].rearrange("p o (m i) -> p o m i", m=2) for d in range(2)]
            rm = upad[:, 4:6, lat].rearrange("p o (m i) -> p o m i", m=2)
            rq = [upad[:, 2 * d:2 * d + 2, 2:2 + CTX] for d in range(2)]
            kvt, qr = xt, ew[:, :, 0:2, :]
            rp = ew[:, :, 2:4, :]
            vtr = [stm[:, b].rearrange("p g i -> p (g i)") for b in range(2)]
            ry, ry2 = (xt[:].rearrange("p c n -> p (c n)")[:, b * 2 * T:(b + 1) * 2 * T]
                       .rearrange("p (m t) -> p m t", m=2) for b in range(2))
            with ExitStack() as part:
                kh = sb("kh", [P, HM, 512], F32, part)
                sb("attention_gap", [P, 6 * CONVT + NCH * 512 - HM * 512], F32, part)
                ck = sb("ck", [P, 512], F32, part)
                kr = sb("kr", [P, 512], F32, part)
                vm = sb("vm", [P, 4, 256], F32, part)
                rt = sb("rt", [P, 2, LAT], F32, part)
                qh = sb("qh", [P, HM, T], F32, part)
            pr, pt = (adas[:, b, 0:2 * T].rearrange("p (b t) -> p b t", b=2) for b in range(2))

        def cc(k, n=P):
            return const[:, k:k + n]

        def sc(k, n=1):
            return small[:, k:k + n]

        def spread(ap, n, shape):
            return ap.unsqueeze(len(shape)).to_broadcast([P, *shape[1:], n])

        def over(ap, n):
            return ap.unsqueeze(1).to_broadcast([ap.shape[0], n, ap.shape[1]])

        ident, ones = cc(K_ID), cc(K_ONE)
        tri = (cc(K_U), cc(K_L))
        after = (cc(K_SL), cc(K_SU))
        eps = cc(K_EPS, 1)
        STATE_JOBS = ((0, 0), (0, 1), (1, 0), (2, 1))

        def beside_ffn(L, j):
            i = nc.s_assert_within(j + L * 2 + (N_F1 // 2 - 4), 1, N_F1 // 2 - 2,
                                   skip_runtime_bounds_check_because="the last layer does one iteration")
            p = nc.s_assert_within(j + L * 6 + 5, 5, 6 * DEPTH - 1,
                                   skip_runtime_bounds_check_because="the last layer does one iteration")
            return i, p, j + L * TURNS + 3

        block = ctx.enter_context(nc.Block())

        @block.sync
        def _(sp):
            def load_ada(p, k, w=1):
                for half in range(w):
                    b = k * w + half
                    sp.wait_ge(ada_used, p * KD + b + 1)
                    sp.dma_start(adas[:, b % 4, :], wada_d[p * KD + b]).then_inc(ada_in[b % 4], 16)

            def load_w(L, n, j, dst, src):
                sp.wait_ge(w_split, L * NB + n + 1)
                sp.dma_start(dst, src).then_inc(stage_in[j], 16)

            sp.dma_start(const[:], const_d).then_inc(const_in, 16)
            sp.dma_start(x[:], x_d).then_inc(x_in, 16)
            with sp.Fori(0, DEPTH) as L:
                load_w(L, 0, 0, stage[:, 0, 0:P], wdt_d[L])
                load_w(L, 1, 1, stage[:, 1, :], win_d[L * (N_WIN - 1)])
                sp.wait_ge(rstd_ready, L * RSTD + 1)
                sp.dma_start(small[:], small_d[L]).then_inc(small_in, 16)
                for n in range(2, N_WIN):
                    load_w(L, n, n % 2, stage[:, n % 2, :], win_d[L * (N_WIN - 1) + (n - 1)])
                    for k in ADA_BESIDE.get(n - 1, ()):
                        load_ada(L * 6 + 2, k)
                    if n == 8:
                        sp.wait_ge(ssd_state, L * 2 + 1)
                        sp.dma_start(sssd_d[L], sout[:].rearrange("p a b -> p (a b)")).then_inc(stored, 16)
                for i in range(2):
                    load_w(L, N_WIN + i, i, stage[:, i, :], wout_d[L * N_WOUT + i])
                for k in range(KD):
                    load_ada(L * 6 + 3, k, 2)
                sp.wait_ge(ret_state, L * 4 + 2)
                sp.dma_start(sret_d[L], rout[:].rearrange("p a b c -> p (a b c)")).then_inc(stored, 16)
                sp.wait_ge(ck_ready, L * 3 + 3)
                sp.dma_start(ckv_d[L], ck[:, 0:CTX]).then_inc(stored, 16)
                sp.dma_start(kr_d[L], u[KR0:KR0 + ROPE, U_KR, 0:CTX]).then_inc(stored, 16)
                for i in range(2, N_WOUT):
                    load_w(L, N_WIN + i, i % 2, stage[:, i % 2, :], wout_d[L * N_WOUT + i])
                for j in range(2):
                    load_w(L, j + N_WIN + N_WOUT, j, stage[:, j, :], wf1_d[L * N_F1 + j])
                def load_up(i):
                    for j in range(2):
                        load_w(L, i * 2 + (j + N_WIN + N_WOUT), j, stage[:, j, :], wf1_d[L * N_F1 + i * 2 + j])

                with sp.Fori(1, L * 2 + (N_F1 // 2 - 4)) as i:
                    load_up(i)
                with sp.Fori(0, 3 - L * 2) as t:
                    i, p, turn = beside_ffn(L, t)
                    load_up(i)
                    sp.wait_ge(rstd_ready, L * RSTD + 7)
                    for k in range(KD):
                        load_ada(p, k)
                load_up(N_F1 // 2 - 1)
                with sp.Fori(0, N_F2 // 2) as i:
                    for j in range(2):
                        load_w(L, i * 2 + (j + N_WIN + N_WOUT + N_F1), j, stage[:, j, 0:F2BLK],
                               wf2_d[L * N_F2 + i * 2 + j])
            for k in range(0, KD, 2):
                sp.wait_ge(y_ready, k + 2)
                sp.dma_start(y_d[:, k:k + 2, :], sq[:, k:k + 2, :]).then_inc(stored, 16)
            sp.wait_ge(stored, 16 * (4 * DEPTH + KD // 2))

        @block.tensor
        def _(pe):
            mm, tp = nc.tensor.matmul, nc.tensor.transpose

            def split_mm(out, lhs, rhs, k, n):
                (ah, al), (bh, bl) = lhs, rhs
                mm(out, ah, bh, start=(k == 0), stop=False)
                mm(out, ah, bl, start=False, stop=False)
                return mm(out, al, bh, start=False, stop=(k == n - 1))

            def wtile(j, t):
                return whi[:, j, t * P:(t + 1) * P], wlo[:, j, t * P:(t + 1) * P]

            def hk(k, a=0, b=T):
                return h_hi[:, k, a:b], h_lo[:, k, a:b]

            def w_ready(L, n):
                pe.wait_ge(w_split, L * NB + n + 3)

            def wide_block(L, n, j):
                w_ready(L, n)
                for s in range(2):
                    for k in range(KD):
                        last = split_mm(ps[:, 2 * j + s, 0:T], wtile(j, 2 * k + s), hk(k), k, KD)
                last.then_inc(w_used, 1)

            def ada_block(p, k, w=1, first=False):
                for half in range(w):
                    b = k * w + half
                    src = adaf[:, b // 4, b % 4] if first and b < 12 else adas[:, b % 4]
                    if not first:
                        pe.wait_ge(ada_in[b % 4], p * 32 + 16 * (b // 4) - 32)
                    elif b % 4 == 0:
                        pe.wait_ge(ada_in[b // 4], 16)
                    for j in range(4):
                        last = mm(ps[j * CW:(j + 1) * CW, 4, half * 256:half * 256 + 256], cond[:, k, :],
                                  src[:, j * 256:(j + 1) * 256], start=(b == 0), stop=(b == w * KD - 1))
                    last.then_inc(ada_used, 1)

            def ada_turn(turn, w=1, bank=4):
                pe.wait_ge(ada_out, turn + 1)
                for i in range(2 * w):
                    last = tp(ps[:, bank, i * P:(i + 1) * P], adac[:, i * P:(i + 1) * P], ident)
                last.then_inc(ada_tr, 1)

            def add_square(first, k, src=None):
                pe.wait_ge(sq_ready, first + (k + 1))
                return mm(ps[:, 7, 0:T], ones, sq[:, k, :] if src is None else src, start=(k == 0), stop=(k == KD - 1))

            pe.sem_inc(w_used, 2)
            pe.sem_inc(ada_used, 4)
            for k in range(KD):
                last = add_square(0, k)
            last.then_inc(ms_ready, 1)
            pe.wait_ge(cond_ready, 1)
            for k in range(KD):
                ada_block(0, k, 2, True)
            ada_turn(0, 2)

            with pe.Fori(0, DEPTH) as L:
                w_ready(L, 1)
                for k in range(KD):
                    pe.wait_ge(h_ready, L * 16 + k + 1)
                    last = split_mm(ps[0:16, 0, 0:T], (dthi[:, k * 16:k * 16 + 16], dtlo[:, k * 16:k * 16 + 16]),
                                    hk(k), k, KD)
                    if k == KD - 1:
                        last.then_inc(w_used, 1)
                    for s in range(2):
                        last = split_mm(ps[:, 2 + s, 0:T], wtile(1, 2 * k + s), hk(k), k, KD)
                last.then_inc(w_used, 1)

                def win_block(n):
                    if n == 2:
                        pe.wait_ge(dt_taken, L + 1)
                    if n >= 3:
                        pe.wait_ge(u_ready, L * (N_WIN - 1) + n - 2)
                    wide_block(L, n, n % 2)
                    for k in ADA_BESIDE.get(n, ()):
                        ada_block(L * 6 + 2, k)

                pe.wait_ge(mod_ready, L * TURNS + 2)
                for k in ADA_BESIDE[1]:
                    ada_block(L * 6 + 2, k)
                win_block(2)
                for c in range(NCH):
                    last = tp(ps[:, 5, c * 16:c * 16 + 16], nt[0:16, 0, c * P:c * P + P], const[0:16, K_ID:K_ID + 16])
                last.then_inc(dt_tr, 1)
                win_block(3)

                pe.wait_ge(loga_ready, L * 2 + 2)
                for d in range(2):
                    mm(ps[:, 5, d * 24:d * 24 + 24], tri[d], loga[:, :, d, :], start=True, stop=True)
                    mm(ps[:, 5, 48 + d * 24:72 + d * 24], after[d], loga[:, :, d, :], start=True, stop=True)
                for c, d in STATE_JOBS[2:]:
                    for g in range(2):
                        last = mm(ps[g * 64:g * 64 + 64, 5, 96 + d * 4:100 + d * 4], ones[:, 0:64],
                                  loga[:, c, d, g * 4:g * 4 + 4], start=True, stop=True)
                last.then_inc(cum_ps, 1)

                win_block(4)
                pe.wait_ge(v_ready, L * 6 + 6)
                pe.wait_ge(cum_ready, L * 3 + 3)

                def turn_values(c, bank):
                    for t in range(4):
                        last = tp(ps[:, bank, t * P:t * P + P], v[:, t, CS[c]:CS[c] + P], ident)
                    last.then_inc(tr_ps, 1)

                turn_values(0, 6)
                turn_values(1, 7)
                for c in range(NCH):
                    last = tp(ps[:, 5, P + c * P:P + c * P + P], v[:, 4, CS[c]:CS[c] + P], ident)
                last.then_inc(tr_ps, 1)
                pe.wait_ge(u_ready, L * (N_WIN - 1) + 4)
                turn_values(2, 0)
                win_block(5)

                pe.wait_ge(tr_ready, L * 4 + 4)
                for s, (c, d) in enumerate(STATE_JOBS):
                    pe.wait_ge(vte_ready, L * 4 + s + 1)
                    for g in range(2):
                        last = mm(ps[g * 64:g * 64 + 64, 6 + s // 2, d * 256:d * 256 + 256],
                                  bt[:, c, g * 64:g * 64 + 64], vte[s][:, g * 256:g * 256 + 256], start=True, stop=True)
                    last.then_inc(st_ps, 1)
                pe.wait_ge(ssd_state, L * 2 + 2)
                for c in range(NCH):
                    for g in range(2):
                        q = 2 * c + g
                        rows = slice(g * 64, g * 64 + 64)
                        if q:
                            pe.wait_ge(stm_ready, L * 12 + 2 * q)
                        mm(ps[:, 7, 0:P], v[rows, 4, CS[c]:CS[c] + P], v[rows, 5, CS[c]:CS[c] + P],
                           start=True, stop=True).then_inc(score_ps, 1)
                        if q:
                            pe.wait_ge(seg_ready, L * 6 + q)
                        if q >= 3:
                            pe.wait_ge(ec_ready, L * 4 + q - 2)
                        for d in range(2):
                            for hh in range(HSG):
                                h = g * HSG + hh
                                last = mm(ps[:, 5 + d, hh * P:hh * P + P],
                                          loga[:, c, d, h:h + 1].to_broadcast([P, P]), tri[d], start=True, stop=True)
                        last.then_inc(row_ps, 1)
                        if q == 0:
                            ada_turn(L * TURNS + 1)
                        win_block(6 + q)
                        if q == 5:
                            pe.wait_ge(seg_ready, L * 6 + 6)
                            pe.wait_ge(ec_ready, L * 4 + 4)
                            pe.wait_ge(stm_ready, L * 12 + 12)
                            for cr in range(NCH):
                                for t in range(4):
                                    last = tp(ps[:, 5 + cr, t * P:t * P + P], u[:, U_RK + t, cr * P:cr * P + P], ident)
                                last.then_inc(kv_ps, 1)
                        if q == 0:
                            pe.wait_ge(mod_ready, L * TURNS + 3)
                        if g == 0 and c:
                            pe.wait_ge(ssd_y, L * 3 + c)
                        pe.wait_ge(vd_ready, L * 6 + 2 * c + 2)
                        if c:
                            pe.wait_ge(qsc_ready, L * 4 + q - 1)
                        pe.wait_ge(prob_ready, L * 12 + 2 * q + 2)
                        for hh in range(HSG):
                            h = g * HSG + hh
                            o = (h % 2) * 64
                            out = ps[o:o + 64, 4, (h // 2) * P:(h // 2) * P + P]
                            for d in range(2):
                                last = mm(out, vd[:, d, h * 64:h * 64 + 64], ew[:, d, hh, :], start=(d == 0),
                                          stop=(d == 1 and c == 0))
                            if c:
                                for d in range(2):
                                    if (c, d) in ((1, 0), (2, 1)):
                                        st = small[rows, C_H0S + d * 256 + hh * 64:C_H0S + d * 256 + hh * 64 + 64]
                                    else:
                                        st = hs[rows, d, hh * 64:hh * 64 + 64]
                                    last = mm(out, st, ec[rows, d, hh, :], start=False, stop=(d == 1))
                        last.then_inc(y_ps, 1)

                def mean_square(n, tiles):
                    pe.wait_ge(gsq_ready, L * 4 + n)
                    for m, src in enumerate(tiles):
                        last = mm(ps[:, 7, 0:T], ones, src, start=(m == 0), stop=(m == len(tiles) - 1))
                    last.then_inc(ms_ready, 1)

                pe.wait_ge(kv_ready, L * 3 + 3)
                for s, (c, d) in enumerate(STATE_JOBS):
                    pe.wait_ge(rvt_ready, L * 4 + s + 1)
                    if s >= 2:
                        pe.wait_ge(ret_state, L * 4 + s - 1)
                    for r in range(HR):
                        o = (r % 2) * 64
                        last = mm(ps[o:o + 64, 5 + s % 2, (r // 2) * 64:(r // 2) * 64 + 64],
                                  kvt[:, c, r * 64:r * 64 + 64], vtr[s % 2][:, r * 64:r * 64 + 64], start=True, stop=True)
                    last.then_inc(rst_ps, 1)
                pe.wait_ge(ssd_y, L * 3 + 3)
                ada_block(L * 6 + 3, 0, 2)
                ada_block(L * 6 + 3, 1, 2)
                pe.wait_ge(ret_state, L * 4 + 4)
                pe.wait_ge(u_ready, L * (N_WIN - 1) + N_WIN - 1)
                for c in range(NCH):
                    if c:
                        pe.wait_ge(rprob_ready, L * 3 + c)
                    for r in range(HR):
                        rows = slice((r % 2) * 64, (r % 2) * 64 + 64)
                        last = mm(ps[:, 2 + r % 2, (r // 2) * P:(r // 2) * P + P], u[rows, U_RK + r // 2, c * P:c * P + P],
                                  u[rows, U_RQ + r // 2, c * P:c * P + P], start=True, stop=True)
                    last.then_inc(rscore_ps, 1)
                    if c:
                        pe.wait_ge(rstd_ready, L * RSTD + 2 + c)
                    mean_square(c + 1, ([gsq[:, m, :] for m in range(4)], [gsq[:, m, :] for m in range(2)],
                                        [gsq[:, 2, :]])[c])
                    ada_block(L * 6 + 3, 2 + c, 2)
                    pe.wait_ge(rprob_ready, L * 3 + c + 1)
                    if c:
                        pe.wait_ge(qr_ready, L * 4 + 2 * c)
                    for r in range(HR):
                        rows = slice((r % 2) * 64, (r % 2) * 64 + 64)
                        m = r // 2
                        out = ps[rows, m, c * P:c * P + P]
                        last = mm(out, kvt[:, c, 256 + r * 64:320 + r * 64], rp[:, r % 2, r // 2, :], start=True, stop=(c == 0))
                        if c:
                            for d in range(2):
                                if (c, d) in ((1, 0), (2, 1)):
                                    st = small[rows, C_H0R + d * 128 + m * 64:C_H0R + d * 128 + m * 64 + 64]
                                else:
                                    st = hr[rows, d, m, :]
                                last = mm(out, st, qr[rows, d, m, :], start=False, stop=(d == 1))
                    last.then_inc(ry_ps, 1)

                hrow = slice(0, NOPE + ROPE)
                perm = const[hrow, K_PERM:K_PERM + NOPE + ROPE]
                mm(ps[hrow, 5, 0:LAT], perm, u[hrow, U_KR, CTX:T], start=True, stop=True).then_inc(krot_ps, 1)
                pe.wait_ge(ry_taken, L + 1)
                for m in range(2):
                    last = mm(ps[:, m, 0:T], cc(K_BD), ry[:, m, :], start=True, stop=True)
                last.then_inc(mu_ps, 1)
                ada_block(L * 6 + 3, 5, 2)
                pe.wait_ge(qn_ready, L * 2 + 2)
                pe.wait_ge(rprob_ready, L * 3 + 3)
                for h in range(HM):
                    if h >= 2:
                        pe.wait_ge(q_taken, L * HM + h - 1)
                    for k in range(2):
                        c0 = C_UQ + k * 384 + h * 96
                        last = mm(ps[0:96, 2 + h % 2, 0:T], small[:, c0:c0 + 96], u[:, U_MQ + k, :],
                                  start=(k == 0), stop=(k == 1))
                    last.then_inc(q_ps, 1)
                pe.wait_ge(centred, L + 1)
                pe.wait_ge(gsq_ready, L * 4 + 4)
                for m in range(2):
                    last = mm(ps[:, m, 0:T], cc(K_BD), ry2[:, m, :], start=True, stop=True)
                last.then_inc(ms_ready, 1)
                ada_block(L * 6 + 3, 6, 2)
                pe.wait_ge(kr_ready, L * 3 + 3)
                pe.wait_ge(q_taken, L * HM + HM)
                for h in range(HM):
                    last = mm(ps[hrow, 5 + h // 2, (h % 2) * LAT:(h % 2) * LAT + LAT], perm, qh[hrow, h, CTX:T],
                              start=True, stop=True)
                    if h % 2:
                        last.then_inc(rot_ps, 1)
                pe.wait_ge(ck_ready, L * 3 + 3)
                for h in range(HM):
                    if h >= 2:
                        pe.wait_ge(k_ready, L * HM + h - 1)
                    c0 = C_UKV + h * 128
                    mm(ps[0:64, 2 + h % 2, 0:512], small[:, c0:c0 + 64], ck[:, 0:512], start=True, stop=True)\
                        .then_inc(k_ps, 1)
                wv = small[:, C_UKV:C_UKV + 512].rearrange("p (h n) -> p h n", h=HM)[:, :, 64:128]
                pe.wait_ge(rstd_ready, L * RSTD + 5)
                for kt in range(4):
                    if kt == 1:
                        pe.wait_ge(k_ready, L * HM + 3)
                    if kt >= 2:
                        pe.wait_ge(vm_ready, L * 4 + kt - 1)
                    mm(ps[:, 2 if kt % 2 else 7, 0:256], ck[:, kt * P:kt * P + P], wv, start=True, stop=True)\
                        .then_inc(vm_ps, 1)
                ada_block(L * 6 + 3, 7, 2)
                pe.wait_ge(q_ready, L * 2 + 2)
                pe.wait_ge(kh_rope, L + 1)
                pe.wait_ge(k_ready, L * HM + HM)
                pe.wait_ge(vm_ready, L * 4 + 4)
                pe.wait_ge(rstd_ready, L * RSTD + 6)

                def wout_tile(half, m, bank):
                    n = N_WIN + 2 * half + m // 4
                    if m % 4 == 0:
                        w_ready(L, n)
                    for k in range(KW2):
                        last = split_mm(ps[:, bank, 0:T], wtile(n % 2, (m % 4) * KW2 + k), hk(half * KW2 + k), k, KW2)
                    last.then_inc(w_used if m % 4 == 3 else wo_ps, 1)

                def keys(c):
                    return (0, 1) if c == 0 else (CTX, 3)

                for i in range(NATT + 3):
                    if i == 2:
                        ada_turn(L * TURNS + 2, 2)
                    if i < NATT:
                        c, h = ATT[i]
                        k0, nk = keys(c)
                        if i >= 2:
                            pe.wait_ge(p_exp, L * NATT + i - 1)
                        mm(ps[:, i % 2, 0:nk * P], qh[0:96, h, c * P:c * P + P], kh[0:96, h, k0:k0 + nk * P],
                           start=True, stop=True).then_inc(s_ps, 1)
                    if 0 <= i - 2 < NATT:
                        a = i - 2
                        nk = keys(ATT[a][0])[1]
                        pe.wait_ge(p_ready, L * NATT + a + 1)
                        if a >= 2:
                            pe.wait_ge(pt_ready, L * NATT + a - 1)
                        for kt in range(nk):
                            last = tp(ps[:, 2 + a % 2, kt * P:kt * P + P], pr[:, a % 2, kt * P:kt * P + P], ident)
                        last.then_inc(pt_ps, 1)
                    if 0 <= i - 3:
                        a = i - 3
                        c, h = ATT[a]
                        k0, nk = keys(c)
                        pe.wait_ge(pt_ready, L * NATT + a + 1)
                        o = (h % 2) * 64
                        for kt in range(nk):
                            last = mm(ps[o:o + 64, 5 + h // 2, c * P:c * P + P], vm[:, k0 // P + kt, h * 64:h * 64 + 64],
                                      pt[:, a % 2, kt * P:kt * P + P], start=(kt == 0), stop=(kt == nk - 1))
                        last.then_inc(my_ps, 1)
                    if 0 <= i - 3 < KD:
                        m = i - 3
                        if m == 0:
                            pe.wait_ge(mix_ready, L * KD + KW2)
                            pe.wait_ge(mod_ready, L * TURNS + 4)
                        if m >= 2:
                            pe.wait_ge(x_ready, L * 24 + m)
                        wout_tile(0, m, 4 if m % 2 else 7)

                pe.wait_ge(mix_ready, L * KD + KD)
                for m in range(KD):
                    if m >= 4:
                        pe.wait_ge(x_ready, L * 24 + 6 + m)
                    wout_tile(1, m, m % 4)
                    if m >= 2:
                        add_square(L * 16 + KD, m - 2)
                for k in (KD - 2, KD - 1):
                    last = add_square(L * 16 + KD, k)
                last.then_inc(ms_ready, 1)

                def ffn_up(i, j):
                    pe.wait_ge(hid_ready, L * N_F1 + i * 2 + (j + 1))
                    wide_block(L, i * 2 + (j + N_WIN + N_WOUT), j)

                pe.wait_ge(hid_ready, L * N_F1 + 1)
                w_ready(L, N_WIN + N_WOUT)
                for k in range(KD):
                    pe.wait_ge(h_ready, L * 16 + KD + k + 1)
                    for s in range(2):
                        last = split_mm(ps[:, s, 0:T], wtile(0, 2 * k + s), hk(k), k, KD)
                last.then_inc(w_used, 1)
                ffn_up(0, 1)
                with pe.Fori(1, L * 2 + (N_F1 // 2 - 4)) as i:
                    for j in range(2):
                        ffn_up(i, j)
                with pe.Fori(0, 3 - L * 2) as t:
                    i, p, turn = beside_ffn(L, t)
                    for j in range(2):
                        for k in range(4 * j, 4 * j + 4):
                            if k == 0:
                                pe.wait_ge(ada_out, turn)
                            ada_block(p, k)
                        ffn_up(i, j)
                    pe.wait_ge(mod_ready, turn + 1)
                    ada_turn(turn, bank=5)
                for j in range(2):
                    ffn_up(N_F1 // 2 - 1, j)

                def ffn_down(i, m, first=False):
                    pe.wait_ge(x_ready, L * 24 + i * 2 + (2 * KD + m))
                    for j in range(2):
                        if first and j:
                            pe.wait_ge(hid_lo_ready, L * KF + KF)
                        w_ready(L, i * 4 + (2 * m + j + N_WIN + N_WOUT + N_F1))
                        for t in range(KH2):
                            k = j * KH2 + t
                            last = split_mm(ps[:, m, 0:T], wtile(j, t), (hid_hi[:, k, :], hid_lo[:, k, :]), k, KF)
                        last.then_inc(w_used, 1)

                def next_square(k, slot, start=False, stop=False):
                    pe.wait_ge(sq_ready, L * 16 + k + (2 * KD + 1))
                    mm(ps[:, 7, 0:T], ones, nv[:, slot, :], start=start, stop=stop)\
                        .then_inc(ms_ready if stop else sq_used, 1)

                pe.wait_ge(hid_lo_ready, L * KF + KH2)
                ffn_down(0, 0, True)
                ffn_down(0, 1)
                next_square(0, 0, start=True)
                with pe.Fori(1, KD // 2) as i:
                    ffn_down(i, 0)
                    next_square(i * 2 - 1, 1)
                    ffn_down(i, 1)
                    next_square(i * 2, 0)
                next_square(KD - 1, 1, stop=True)

        @block.scalar
        def _(act):
            f = nc.scalar.activation

            def split_hi(L, n, j, width=BLK):
                act.wait_ge(w_used, L * NB + n + 1)
                act.wait_ge(stage_in[j], in_stage(L, n))
                f(whi[:, j, 0:width], stage[:, j, 0:width], ACT.Copy).then_inc(w_hi, 1)

            def in_stage(L, n):
                if isinstance(n, tuple):
                    i, k = n
                    return L * (16 * NB // 2) + i * 16 + 16 * (k // 2 + 1)
                return L * (16 * NB // 2) + 16 * (n // 2 + 1)

            def split_hi_at(L, i, k, j, width=BLK):
                act.wait_ge(w_used, L * NB + i * 2 + (k + 1))
                act.wait_ge(stage_in[j], in_stage(L, (i, k)))
                f(whi[:, j, 0:width], stage[:, j, 0:width], ACT.Copy).then_inc(w_hi, 1)

            def rstd(val, src, width, inv):
                act.wait_ge(ms_ready, val)
                act.wait_ge(rstd_ready, val)
                y = ny[:, 0:width, :]
                f(y, src, ACT.Ln, bias=eps, scale=inv).then_inc(ln_ready, 1)
                act.wait_ge(ln_ready, val)
                f(y, y, ACT.Exp, scale=-0.5).then_inc(y0_ready, 1)

            def square(k):
                f(sq[:, k, :], x[:, k, :], ACT.Square).then_inc(sq_ready, 1)

            def modulate(L, half):
                a, b = (8, 0) if half == 0 else (32, 24)
                act.wait_ge(fact1 if half == 0 else fact2, L * 2 + 2)

                for k in range(KD):
                    act.wait_ge(xn_ready, L * 16 + (half * KD + k + 1))
                    for st, t0, t1 in ((1, CTX, T), (0, 0, CTX))[:1 + k % 2]:
                        f(sq[:, k, t0:t1], sq[:, k, t0:t1], ACT.Identity, bias=modl[:, b + k, st:st + 1],
                          scale=modl[:, a + k, st:st + 1]).then_inc(h_whole, 1)
                    act.wait_ge(h_whole, L * 32 + half * 16 + 2 * k + 2)
                    f(h_hi[:, k, :], sq[:, k, :], ACT.Copy).then_inc(h_hi_ready, 1)
                    if half == 1 and k == 3:
                        split_hi(L, N_WIN + 5, 1)
                    if half == 0 and k == 3:
                        act.wait_ge(stage_in[0], in_stage(L, 2))
                        f(whi[:, 0, :], stage[:, 0, :], ACT.Copy).then_inc(w_hi, 1)

            def ffn_tile(L, i, j, width):
                act.wait_ge(w_used, L * NB + i * 2 + (j + N_WIN + N_WOUT + 3))
                act.wait_ge(hid_ready, L * N_F1 + i * 2 + (j + 1))
                f(ny[:, j, :], ps[:, 2 * j, 0:T], ACT.Silu).then_inc(silu_ready, 1)
                split_hi_at(L, i, N_WIN + N_WOUT + j + 2, j, width)
                act.wait_ge(hid_ready, L * N_F1 + i * 2 + (j + 3))
                f(hid_hi[:, bass.ds(i * 2 + j, 1), :], nt[:, j:j + 1, :], ACT.Copy).then_inc(hid_hi_ready, 1)

            def mix_high(L, k, src):
                if k < 6:
                    act.wait_ge(mix_src, L * 6 + k + 1)
                f(h_hi[:, k, :], src, ACT.Copy).then_inc(mix_hi, 1)

            def use_exp_and_ln():
                nc.scalar.preload_act_table_set("natural_log_exp_and_others")

            for b in range(4):
                act.dma_start(adaf[:, b] if b < 3 else adas[:],
                              wada_d[4 * b:4 * b + 4].rearrange("b p n -> p b n")).then_inc(ada_in[b], 16)
            act.wait_ge(const_in, 16)
            act.wait_ge(zeroed, 2)
            f(cond[:, :, 0:2], cc(K_COND, 2 * KD).rearrange("p (k s) -> p k s", s=2), ACT.Silu).then_inc(cond_ready, 1)

            act.wait_ge(x_in, 16)
            for k in range(KD):
                square(k)

            use_exp_and_ln()
            with act.Fori(0, DEPTH) as L:
                act.wait_ge(w_used, L * NB + 1)
                act.wait_ge(stage_in[0], in_stage(L, 0))
                f(dthi[:], stage[:, 0, 0:P], ACT.Copy).then_inc(w_hi, 1)
                rstd(L * RSTD + 1, ps[:, 7:8, 0:T], 1, 1.0 / D)
                split_hi(L, 1, 1)
                modulate(L, 0)
                def silu_channels(t):
                    act.wait_ge(conv_ready, L * 6 + t + 1)
                    f(v[:, t, :], v[:, t, :], ACT.Silu, bias=sc(C_CB + t)).then_inc(v_ready, 1)

                def win_out(n):
                    act.wait_ge(w_used, L * NB + n + 3)
                    if n:
                        b = 2 * (n % 2)
                        if n <= 3:
                            f(upad[:, 2 * n - 2:2 * n, 2:2 + CTX], ps[:, b:b + 2, 0:CTX], ACT.Copy)
                            last = f(upad[:, 2 * n - 2:2 * n, LATC + 2:LATC + 2 + LAT], ps[:, b:b + 2, CTX:T], ACT.Copy)
                        elif n == 8:
                            f(u[:, U_CKV, :], ps[:, b, 0:T], ACT.Copy)
                            last = f(u[:, U_KR, :], ps[:, b + 1, 0:T], ACT.Copy)
                        else:
                            last = f(u[:, 2 * n - 8:2 * n - 6, :], ps[:, b:b + 2, 0:T], ACT.Copy)
                        last.then_inc(u_ready, 1)
                    if 0 < n < N_WIN - 1:
                        split_hi(L, n + 2, n % 2)

                win_out(0)
                f(expa[:], sc(C_ALOG, 16), ACT.Exp).then_inc(exps_ready, 1)
                win_out(1)
                win_out(2)
                act.wait_ge(abs_ready, L + 1)
                f(sps[:], spp[:], ACT.Exp, scale=-1.0).then_inc(exps_ready, 1)
                win_out(3)
                act.wait_ge(cum_ps, L + 1)
                f(cum[:].rearrange("p d c h -> p (d c h)"), ps[:, 5, 0:48], ACT.Copy).then_inc(cum_ready, 1)
                f(tedt[:].rearrange("p d c h -> p (d c h)"), ps[:, 5, 48:96], ACT.Exp).then_inc(cum_ready, 1)
                f(cd[:].rearrange("p d h -> p (d h)"), ps[:, 5, 96:104], ACT.Exp).then_inc(cum_ready, 1)
                for t in range(6):
                    silu_channels(t)
                use_exp_and_ln()
                win_out(4)
                for c in range(2):
                    act.wait_ge(tr_ps, L * 4 + c + 1)
                    f(xt[:, c, :], ps[:, 6 + c, :], ACT.Copy).then_inc(tr_ready, 1)
                act.wait_ge(tr_ps, L * 4 + 3)
                f(bt[:].rearrange("p c n -> p (c n)"), ps[:, 5, P:P + T], ACT.Copy).then_inc(tr_ready, 1)
                act.wait_ge(tr_ps, L * 4 + 4)
                f(xt[:, 2, :], ps[:, 0, :], ACT.Copy).then_inc(tr_ready, 1)
                win_out(5)
                for c in range(NCH):
                    for g in range(2):
                        q = 2 * c + g
                        if c:
                            rows = slice(g * 64, g * 64 + 64)
                            act.wait_ge(row_ps, L * 6 + q + 1)
                            act.wait_ge(y_ps, L * 6 + q)
                            f(ec[rows].rearrange("p d h i -> p d (h i)"), ps[rows, 5:7, :], ACT.Exp)\
                                .then_inc(ec_ready, 1)
                        act.wait_ge(seg_ready, L * 6 + q + 1)
                        w = ew[:].rearrange("p d h i -> p (d h i)")
                        f(w, w, ACT.Exp).then_inc(e_ready, 1)
                        if q == 5:
                            for cr in range(NCH):
                                act.wait_ge(kv_ps, L * 3 + cr + 1)
                                f(kvt[:, cr, :], ps[:, 5 + cr, :], ACT.Copy).then_inc(kv_ready, 1)
                        win_out(6 + q)
                        if q == 0:
                            for d in range(2):
                                for r in range(HR):
                                    f(rmt[d][:, r % 2, r // 2, :], cc((K_PF, K_PB)[d]), ACT.Exp,
                                      scale=lg[:, d * HR + r:d * HR + r + 1])
                                for m in range(2):
                                    f(rq[d][:, m, :], cc((K_IP, K_IB)[d]), ACT.Exp,
                                      scale=lg[:, 8 + 2 * m + d:9 + 2 * m + d])
                                f(ter[:, d, :], lg[:, d * HR:d * HR + HR], ACT.Exp, scale=cc(K_PC + d, 1))
                            f(cdr[:], lg[:, 8:12], ACT.Exp, scale=float(P)).then_inc(rexp_ready, 1)
                act.wait_ge(u_ready, L * (N_WIN - 1) + N_WIN - 1)
                f(u[:, U_Z:U_Z + 6, :], u[:, U_Z:U_Z + 6, :], ACT.Silu).then_inc(gates_ready, 1)
                use_exp_and_ln()
                act.wait_ge(ssd_gated, L * 2 + 2)
                f(gsq[:], u[:, U_Z:U_Z + 4, :], ACT.Square).then_inc(gsq_ready, 1)
                rrow = slice(KR0, KR0 + ROPE)
                f(ck[:, P:2 * P], sc(C_CKV, P), ACT.Copy).then_inc(ck_ready, 1)
                f(kr[rrow, 0:CTX], u[rrow, U_KR, 0:CTX], ACT.Copy).then_inc(kr_ready, 1)
                f(kr[rrow, CTX:2 * P], small[rrow, C_KR:C_KR + P], ACT.Copy).then_inc(kr_ready, 1)
                split_hi(L, N_WIN + 1, 1)
                rstd(L * RSTD + 2, ps[:, 7:8, 0:T], 1, 1.0 / (HS * 64))
                f(gsq[:, 0:2, :], u[:, U_MQ:U_MQ + 2, :], ACT.Square).then_inc(gsq_ready, 1)
                f(gsq[:, 2, :], u[:, U_CKV, :], ACT.Square).then_inc(gsq_ready, 1)
                act.wait_ge(w_used, L * NB + N_WIN + 2)
                for k in range(4):
                    mix_high(L, k, u[:, U_Z + k, :])
                rstd(L * RSTD + 3, ps[:, 7:8, 0:T], 1, 1.0 / RANKQ)
                rstd(L * RSTD + 4, ps[:, 7:8, 0:T], 1, 1.0 / RANKKV)
                for h in range(HM):
                    act.wait_ge(q_ps, L * HM + h + 1)
                    f(qh[0:96, h, :], ps[0:96, 2 + h % 2, 0:T], ACT.Copy).then_inc(q_taken, 1)
                    if h == 1:
                        act.wait_ge(centred, L + 1)
                        f(ry2[:], ry[:], ACT.Square).then_inc(gsq_ready, 1)
                rstd(L * RSTD + 5, ps[:, 0:2, 0:T], 2, 1.0)
                for h in range(HM):
                    act.wait_ge(k_ps, L * HM + h + 1)
                    f(kh[0:64, h, :], ps[0:64, 2 + h % 2, 0:512], ACT.Copy).then_inc(k_ready, 1)
                for kt in range(4):
                    act.wait_ge(vm_ps, L * 4 + kt + 1)
                    f(vm[:, kt, :], ps[:, 2 if kt % 2 else 7, 0:256], ACT.Copy).then_inc(vm_ready, 1)
                for i in range(NATT + 2):
                    if i < NATT:
                        nk = 1 if ATT[i][0] == 0 else 3
                        act.wait_ge(max_ready, L * NATT + i + 1)
                        if i >= 2:
                            act.wait_ge(pt_ps, L * NATT + i - 1)
                        f(pr[:, i % 2, 0:nk * P], ps[:, i % 2, 0:nk * P], ACT.Exp, bias=att[:, 1, i:i + 1], scale=SCALE,
                          accum_out=att[:, 2, i:i + 1]).then_inc(p_exp, 1)
                    if i >= 2:
                        a = i - 2
                        nk = 1 if ATT[a][0] == 0 else 3
                        act.wait_ge(pt_ps, L * NATT + a + 1)
                        if a >= 2:
                            act.wait_ge(my_ps, L * NATT + a - 1)
                        f(pt[:, a % 2, 0:nk * P], ps[:, 2 + a % 2, 0:nk * P], ACT.Copy).then_inc(pt_ready, 1)
                    if i == 4:
                        for k in range(2):
                            mix_high(L, 4 + k, ry[:, k, :])
                    if i == 8:
                        split_hi(L, N_WIN + 2, 0)
                    if i == 12:
                        split_hi(L, N_WIN + 3, 1)
                act.wait_ge(my_ps, L * NATT + NATT)
                for k in range(2):
                    mix_high(L, 6 + k, ps[:, 5 + k, 0:T])
                act.wait_ge(stored, L * 64 + 64)
                for k in range(KD):
                    act.wait_ge(x_ready, L * 24 + k + 2 + KD)
                    square(k)
                    if k == 3:
                        split_hi(L, N_WIN + 4, 0)
                rstd(L * RSTD + 6, ps[:, 7:8, 0:T], 1, 1.0 / D)
                modulate(L, 1)
                nc.scalar.preload_act_table(ACT.Silu)
                with act.Fori(0, N_F1 // 2 - 1) as i:
                    for j in range(2):
                        ffn_tile(L, i, j, BLK)
                for j in range(2):
                    ffn_tile(L, N_F1 // 2 - 1, j, F2BLK)
                def down_split(i, m):
                    for j in range(2):
                        k = 2 * m + j + N_WIN + N_WOUT + N_F1
                        act.wait_ge(w_used, L * NB + i * 4 + (k + 3))
                        act.wait_ge(stage_in[j], L * (16 * NB // 2) + i * 32 + 16 * (k // 2 + 2))
                        f(whi[:, j, 0:F2BLK], stage[:, j, 0:F2BLK], ACT.Copy).then_inc(w_hi, 1)

                def down_square(i, m, first=False):
                    act.wait_ge(x_ready, L * 24 + i * 2 + (m + 2 + 2 * KD))
                    if not first:
                        act.wait_ge(sq_used, L * (KD - 1) + i * 2 + (m - 1))
                    f(nv[:, m, :], x[:, bass.ds(i * 2 + m, 1), :].rearrange("p o t -> p (o t)"), ACT.Square)\
                        .then_inc(sq_ready, 1)

                use_exp_and_ln()
                for m in range(2):
                    down_split(0, m)
                    down_square(0, m, True)
                with act.Fori(1, KD // 2 - 1) as i:
                    for m in range(2):
                        down_split(i, m)
                        down_square(i, m)
                down_split(KD // 2 - 1, 0)
                down_square(KD // 2 - 1, 0)
                down_square(KD // 2 - 1, 1)
            rstd(RSTD * DEPTH + 1, ps[:, 7:8, 0:T], 1, 1.0 / D)

        @block.vector
        def _(dve):
            steps = [0]
            tt, ts, stt = nc.vector.tensor_tensor, nc.vector.tensor_scalar, nc.vector.scalar_tensor_tensor

            def step(L, ins):
                steps[0] += 1
                ins.then_inc(dve_step, 1)
                dve.wait_ge(dve_step, (0 if L is None else L * DVE_STEPS) + steps[0])

            def split_lo(L, n, j, width=BLK):
                if isinstance(n, tuple):
                    dve.wait_ge(w_hi, L * NB + n[0] * 2 + (n[1] + 1))
                else:
                    dve.wait_ge(w_hi, L * NB + (n + 1))
                tt(wlo[:, j, 0:width], stage[:, j, 0:width], whi[:, j, 0:width].bitcast(F32), ALU.subtract)\
                    .then_inc(w_split, 1)

            def ada_rows(p, w=1):
                dve.wait_ge(ada_used, p * KD + w * KD + 4)
                nc.vector.tensor_copy(adac[:, 0:w * 256], ps[:, 4, 0:w * 256]).then_inc(ada_out, 1)

            def ada_mod(turn, p, w=1, bank=4):
                dve.wait_ge(ada_tr, turn + 1)
                for half in range(w):
                    for st in range(2):
                        t0 = (p + half) * PART_TILES
                        last = nc.vector.tensor_tensor(
                            mod[:, bass.ds(t0, PART_TILES), st].rearrange("p (j i) -> p j i", j=4),
                            ps[:, bank, half * 256:half * 256 + 256].rearrange("p (i j w) -> p j i w", i=2, j=4)[:, :, :, st],
                            const[:, bass.ds(t0 + K_BADA, PART_TILES)].rearrange("p (j i) -> p j i", j=4), ALU.add)
                last.then_inc(mod_ready, 1)

            def rstd(L, val, src, width, inv):
                n, y, t = nv[:, 0:width, :], ny[:, 0:width, :], nt[:, 0:width, :]
                dve.wait_ge(ln_ready, val)
                ts(n, src, -0.5 * inv, -0.5 * EPS, ALU.mult, ALU.add)
                dve.wait_ge(y0_ready, val)
                step(L, tt(t, y, y, ALU.mult))
                step(L, tt(t, t, n, ALU.mult))
                stt(n, t, 1.5, y, ALU.add, ALU.mult).then_inc(rstd_ready, 1)
                dve.wait_ge(rstd_ready, val + 1)

            def normed(L, half):
                def scaled(k):
                    tt(sq[:, k, :], x[:, k, :], nv[:, 0, :], ALU.mult).then_inc(xn_ready, 1)

                a, b = (8, 0) if half == 0 else (32, 24)
                scaled(0)
                scaled(1)
                for k in range(KD):
                    if k % 2 == 0:
                        dve.wait_ge(xn_ready, L * 16 + (half * KD + k + 1))
                        ts(sq[:, k, 0:CTX], sq[:, k, 0:CTX], modl[:, a + k, 0:1], modl[:, b + k, 0:1], ALU.mult,
                           ALU.add).then_inc(h_whole, 1)
                    if k + 2 < KD:
                        scaled(k + 2)
                    if k == KD - 1:
                        dve.wait_ge(w_split, L * NB + (2 if half == 0 else N_WIN + 5) + 3)
                    dve.wait_ge(h_hi_ready, L * 16 + (half * KD + k + 1))
                    tt(h_lo[:, k, :], sq[:, k, :], h_hi[:, k, :].bitcast(F32), ALU.subtract).then_inc(h_ready, 1)

            def mix_low(L, k, src):
                dve.wait_ge(mix_hi, L * KD + k + 1)
                tt(h_lo[:, k, :], src, h_hi[:, k, :].bitcast(F32), ALU.subtract).then_inc(mix_ready, 1)

            def residual(L, bank, m, gate):
                for s, (t0, t1) in enumerate(((0, CTX), (CTX, T))):
                    xm = x[:, m:m + 1, t0:t1] if isinstance(m, int) else x[:, bass.ds(m, 1), t0:t1]
                    gm = modl[:, gate + m, s:s + 1] if isinstance(m, int) else modl[:, bass.ds(m + gate, 1), s]
                    last = stt(xm, ps[:, bank:bank + 1, t0:t1], gm, xm, ALU.mult, ALU.add)
                last.then_inc(x_ready, 1)

            def wout_residual(L, half, m, bank):
                if m % 4 == 3:
                    dve.wait_ge(w_used, L * NB + N_WIN + 2 * half + m // 4 + 3)
                else:
                    dve.wait_ge(wo_ps, L * 12 + half * 6 + m // 4 * 3 + m % 4 + 1)
                residual(L, bank, m, 16)

            def mixer_gates(L):
                dve.wait_ge(mod_ready, L * TURNS + 3)
                nc.vector.tensor_copy(modl[:, 16:24, :], mod[:, base(L, 16), :]).then_inc(gate1_ready, 1)
                dve.wait_ge(gate1_ready, L + 1)

            def base(L, k):
                return bass.ds(L * 48 + k, 8)

            nc.vector.memset(cond[:], 0.0).then_inc(zeroed, 1)
            nc.vector.memset(upad[:], 0.0).then_inc(zeroed, 1)
            dve.wait_ge(const_in, 16)
            dve.wait_ge(x_in, 16)
            dve.sem_inc(x_ready, 1)
            dve.sem_inc(mod_ready, 1)
            dve.sem_inc(rstd_ready, 1)
            dve.sem_inc(w_split, 2)
            dve.sem_inc(hid_ready, 2)
            ada_rows(0, 2)
            ada_mod(0, 0, 2)

            with dve.Fori(0, DEPTH) as L:
                dve.wait_ge(w_hi, L * NB + 1)
                tt(dtlo[:], stage[:, 0, 0:P], dthi[:].bitcast(F32), ALU.subtract).then_inc(w_split, 1)
                rstd(L, L * RSTD + 1, ps[:, 7:8, 0:T], 1, 1.0 / D)
                dve.wait_ge(small_in, L * 16 + 16)
                dve.wait_ge(mod_ready, L * TURNS + 2)
                nc.vector.tensor_copy(modl[:, 0:8, :], mod[:, base(L, 0), :]).then_inc(fact1, 1)
                stt(modl[:, 8:16, :], mod[:, base(L, 8), :], 1.0, spread(sc(C_N1, KD), 2, [P, KD]), ALU.add, ALU.mult)\
                    .then_inc(fact1, 1)
                dve.wait_ge(fact1, L * 2 + 2)
                normed(L, 0)

                ts(spx[:, 48:60], sc(C_LGB, 12), -1.0, None, ALU.mult)
                def conv_pair(t):
                    dve.wait_ge(u_ready, L * (N_WIN - 1) + t // 2 + 1)
                    for w in range(CONVW):
                        for a in (t, t + 1):
                            xin, wc = upad[:, a, w:w + CONVT], sc(C_CW + w * 6 + a)
                            if w == 0:
                                ins = ts(v[:, a, :], xin, wc, None, ALU.mult)
                            else:
                                ins = stt(v[:, a, :], xin, wc, v[:, a, :], ALU.mult, ALU.add)
                            if w == CONVW - 1:
                                ins.then_inc(conv_ready, 1)
                            elif a == t + 1:
                                step(L, ins)

                dve.wait_ge(w_used, L * NB + 3)
                nc.vector.tensor_copy(nt[0:16, 0, :], ps[0:16, 0, 0:T]).then_inc(dt_taken, 1)
                split_lo(L, 3, 1)
                conv_pair(0)
                dve.wait_ge(dt_tr, L + 1)
                step(L, tt(spx[:, 0:48].rearrange("p (c n) -> p c n", c=NCH),
                           ps[:, 5, 0:48].rearrange("p (c n) -> p c n", c=NCH), over(sc(C_DTB, 16), NCH), ALU.add))
                stt(spp[:], spx[:], -1.0, spx[:], ALU.mult, ALU.max).then_inc(abs_ready, 1)
                dve.wait_ge(exps_ready, L * 2 + 2)
                step(L, ts(spq[:], sps[:], 2.0, None, ALU.add))
                step(L, nc.vector.reciprocal(spq[:], spq[:]))
                step(L, tt(sps[:], sps[:], spq[:], ALU.mult))
                step(L, tt(spq[:], sps[:], sps[:], ALU.mult))
                step(L, ts(spp[:], spq[:], 1.0 / 15, None, ALU.mult))
                for odd in (13, 11, 9, 7, 5, 3):
                    step(L, stt(spp[:], spp[:], 1.0 / odd, spq[:], ALU.add, ALU.mult))
                ts(spx[:], spx[:], 0.0, None, ALU.max)
                step(L, stt(spp[:], spp[:], 1.0, sps[:], ALU.add, ALU.mult))
                step(L, stt(dts[:], spp[:], 2.0, spx[:], ALU.mult, ALU.add))
                stt(loga[:].rearrange("p c d h -> p c (d h)"), dts[:, 0:48].rearrange("p (c n) -> p c n", c=NCH), -1.0,
                    over(expa[:], NCH), ALU.mult, ALU.mult).then_inc(loga_ready, 1)
                ts(lg[:], dts[:, 48:60], -1.0, None, ALU.mult).then_inc(loga_ready, 1)

                conv_pair(2)
                conv_pair(4)
                dve.wait_ge(cum_ready, L * 3 + 3)
                for d in range(2):
                    tt(tedt[:, d], tedt[:, d], dts[:, 0:48].rearrange("p (c d h) -> p d c h", c=NCH, d=2)[:, d],
                       ALU.mult).then_inc(tedt_ready, 1)
                dve.wait_ge(w_split, L * NB + 5 + 3)
                split_lo(L, 6, 0)
                h4 = "p (d h n) -> p (d h) n"
                tt(hs[:].rearrange("p d (h n) -> p (d h) n", h=HSG), sc(C_H0S, 512).rearrange(h4, d=2, h=HSG),
                   spread(cd[:].rearrange("p d h -> p (d h)"), 64, [P, 2 * HSG]), ALU.mult).then_inc(hs_decayed, 1)
                dve.wait_ge(st_ps, L * 4 + 2)
                nc.vector.tensor_copy(sout[:].rearrange("p d n -> p (d n)"), ps[:, 6, :]).then_inc(ssd_state, 1)
                dve.wait_ge(st_ps, L * 4 + 4)
                dve.wait_ge(hs_decayed, L + 1)
                hf = hs[:].rearrange("p d n -> p (d n)")
                tt(hf, hf, ps[:, 7, :], ALU.add).then_inc(ssd_state, 1)
                split_lo(L, 7, 1)
                ada_rows(L * 6 + 2)

                def skip(c):
                    dve.wait_ge(y_ps, L * 6 + 2 * c + 2)
                    for m in range(4):
                        vin = v[:, m, CS[c]:CS[c] + P]
                        last = stt(vin, vin, sc(C_DSK + m), ps[:, 4, m * P:m * P + P], ALU.mult, ALU.add)
                    last.then_inc(ssd_y, 1)

                for c in range(NCH):
                    for g in range(2):
                        q = 2 * c + g
                        dve.wait_ge(score_ps, L * 6 + q + 1)
                        for d in range(2):
                            tt(stm[:, d, g, :], ps[:, 7, 0:P], tri[d], ALU.mult).then_inc(stm_ready, 1)
                        dve.wait_ge(row_ps, L * 6 + q + 1)
                        if q:
                            dve.wait_ge(y_ps, L * 6 + q)
                        if c:
                            dve.wait_ge(ec_ready, L * 4 + q - 1)
                        for d in range(2):
                            for hh in range(HSG):
                                h = g * HSG + hh
                                last = ts(ew[:, d, hh, :], ps[:, 5 + d, hh * P:hh * P + P], cum[:, d, c, h:h + 1], 0.0,
                                          ALU.subtract, ALU.min)
                        last.then_inc(seg_ready, 1)
                        if q == 0:
                            ada_mod(L * TURNS + 1, L * 6 + 2)
                        if c and g == 0:
                            skip(c - 1)
                        if c:
                            rows = slice(g * 64, g * 64 + 64)
                            w = ec[rows].rearrange("p d h i -> p (d h) i")
                            tt(w, w, over(v[rows, 5, CS[c]:CS[c] + P], 2 * HSG), ALU.mult).then_inc(qsc_ready, 1)
                        dve.wait_ge(e_ready, L * 6 + q + 1)
                        dve.wait_ge(stm_ready, L * 12 + 2 * q + 2)
                        for d in range(2):
                            tt(ew[:, d], ew[:, d], over(stm[:, d, g, :], HSG), ALU.mult).then_inc(prob_ready, 1)
                        if q < 5:
                            split_lo(L, 8 + q, q % 2)
                        if q == 4:
                            dve.wait_ge(rexp_ready, L + 1)
                            for d in range(2):
                                for o in range(2):
                                    last = stt(rmt[d][:, o], rmt[d][:, o], 0.125, over(tri[d], 2), ALU.mult, ALU.mult)
                            step(L, last)
                            tt(rm, rmt[0], rmt[1], ALU.add).then_inc(rmat_ready, 1)
                            ts(ter[:], ter[:], 0.125, None, ALU.mult).then_inc(rmat_ready, 1)
                skip(NCH - 1)

                def ret_end(s):
                    c, d = STATE_JOBS[s]
                    dve.wait_ge(rst_ps, L * 4 + s + 1)
                    bank = ps[:, 5 + s % 2, 0:128].rearrange("p (m n) -> p m n", m=2)
                    if s < 2:
                        last = nc.vector.tensor_copy(rout[:, d], bank)
                    else:
                        for m in range(2):
                            last = stt(hr[:, d, m, :], sc(C_H0R + d * 128 + m * 64, 64), cdr[:, 2 * m + d:2 * m + d + 1],
                                       bank[:, m, :], ALU.mult, ALU.add)
                    last.then_inc(ret_state, 1)

                def ret_probs(c):
                    dve.wait_ge(rscore_ps, L * 3 + c + 1)
                    if c:
                        dve.wait_ge(ry_ps, L * 3 + c)
                    tt(rp[:], ps[:, 2:4, 0:256].rearrange("p o (m i) -> p o m i", m=2), rm, ALU.mult)\
                        .then_inc(rprob_ready, 1)

                ret_end(0)
                ret_end(1)
                dve.wait_ge(ssd_y, L * 3 + 3)
                dve.wait_ge(gates_ready, L + 1)
                for c0, t0, t1 in ((0, 0, CTX), (LATC, CTX, T)):
                    z = u[:, U_Z:U_Z + 4, t0:t1]
                    tt(z, z, v[:, 0:4, c0:c0 + t1 - t0], ALU.mult).then_inc(ssd_gated, 1)
                ret_end(2)
                ret_end(3)
                dve.wait_ge(rmat_ready, L * 2 + 2)
                ret_probs(0)
                split_lo(L, N_WIN + 1, 1)
                rstd(L, L * RSTD + 2, ps[:, 7:8, 0:T], 1, 1.0 / (HS * 64))
                for m in range(4):
                    z = u[:, U_Z + m, :]
                    stt(z, z, sc(C_SN + m), nv[:, 0, :], ALU.mult, ALU.mult).then_inc(mix_src, 1)
                ret_probs(1)
                dve.wait_ge(mix_src, L * 6 + 4)
                rstd(L, L * RSTD + 3, ps[:, 7:8, 0:T], 1, 1.0 / RANKQ)
                for m in range(2):
                    q = u[:, U_MQ + m, :]
                    stt(q, q, sc(C_QN + m), nv[:, 0, :], ALU.mult, ALU.mult).then_inc(qn_ready, 1)
                ret_probs(2)
                for m in range(4):
                    mix_low(L, m, u[:, U_Z + m, :])
                dve.wait_ge(qn_ready, L * 2 + 2)
                dve.wait_ge(ry_ps, L * 3 + 3)
                nc.vector.tensor_copy(ry[:], ps[:, 0:2, 0:T]).then_inc(ry_taken, 1)
                rstd(L, L * RSTD + 4, ps[:, 7:8, 0:T], 1, 1.0 / RANKKV)
                for k0, t0, t1 in ((0, 0, CTX), (2 * P, CTX, T)):
                    stt(ck[:, k0:k0 + t1 - t0], u[:, U_CKV, t0:t1], sc(C_KN), nv[:, 0, t0:t1], ALU.mult, ALU.mult)\
                        .then_inc(ck_ready, 1)
                dve.wait_ge(mu_ps, L + 1)
                tt(ry[:], ry[:], ps[:, 0:2, 0:T], ALU.subtract).then_inc(centred, 1)
                rrow = slice(KR0, KR0 + ROPE)
                cos, sin = const[rrow, K_COS:K_COS + LAT], const[rrow, K_SIN:K_SIN + LAT]
                dve.wait_ge(krot_ps, L + 1)
                tt(rt[rrow, 0, :], ps[rrow, 5, 0:LAT], sin, ALU.mult)
                step(L, tt(kr[rrow, 256:512], u[rrow, U_KR, CTX:T], cos, ALU.mult))
                tt(kr[rrow, 256:512], kr[rrow, 256:512], rt[rrow, 0, :], ALU.add).then_inc(kr_ready, 1)
                dve.wait_ge(kr_ready, L * 3 + 3)
                nc.vector.tensor_copy(kh[rrow, :, :], over(kr[rrow, :], HM)).then_inc(kh_rope, 1)
                mixer_gates(L)
                for hp in range(2):
                    dve.wait_ge(rot_ps, L * 2 + hp + 1)
                    if hp:
                        dve.wait_ge(q_ready, L * 2 + hp)
                    q = qh[rrow, 2 * hp:2 * hp + 2, CTX:T]
                    tt(rt[rrow], ps[rrow, 5 + hp, :].rearrange("p (h t) -> p h t", h=2), over(sin, 2), ALU.mult)
                    step(L, tt(q, q, over(cos, 2), ALU.mult))
                    tt(q, q, rt[rrow], ALU.add).then_inc(q_ready, 1)
                dve.wait_ge(ck_ready, L * 3 + 3)
                rstd(L, L * RSTD + 5, ps[:, 0:2, 0:T], 2, 1.0)
                ada_rows(L * 6 + 3, 2)
                for i in range(NATT + 1):
                    if i in (1, 2):
                        m = i - 1
                        step(L, stt(ry[:, m, :], ry[:, m, :], sc(C_GN + m), nv[:, m, :], ALU.mult, ALU.mult))
                        tt(ry[:, m, :], ry[:, m, :], u[:, U_G + m, :], ALU.mult).then_inc(mix_src, 1)
                    if i == 3:
                        ada_mod(L * TURNS + 2, L * 6 + 3, 2)
                    if i in (5, 6):
                        mix_low(L, i - 1, ry[:, i - 5, :])
                    if i < NATT:
                        nk = 1 if ATT[i][0] == 0 else 3
                        dve.wait_ge(s_ps, L * NATT + i + 1)
                        step(L, nc.vector.reduce_max(att[:, 0, i:i + 1], ps[:, i % 2, 0:nk * P], AX_X))
                        ts(att[:, 1, i:i + 1], att[:, 0, i:i + 1], -SCALE, None, ALU.mult).then_inc(max_ready, 1)
                    if i >= 1:
                        a = i - 1
                        nk = 1 if ATT[a][0] == 0 else 3
                        dve.wait_ge(p_exp, L * NATT + a + 1)
                        step(L, nc.vector.reciprocal(att[:, 3, a:a + 1], att[:, 2, a:a + 1]))
                        w = pr[:, a % 2, 0:nk * P]
                        ts(w, w, att[:, 3, a:a + 1], None, ALU.mult).then_inc(p_ready, 1)
                    if 0 <= i - 4 < KD:
                        wout_residual(L, 0, i - 4, 7 if i % 2 == 0 else 4)
                    if i == 8:
                        split_lo(L, N_WIN + 2, 0)
                for k in range(2):
                    mix_low(L, 6 + k, ps[:, 5 + k, 0:T])

                split_lo(L, N_WIN + 3, 1)
                dve.wait_ge(mod_ready, L * TURNS + 4)
                nc.vector.tensor_copy(modl[:, 24:32, :], mod[:, base(L, 24), :]).then_inc(fact2, 1)
                stt(modl[:, 32:40, :], mod[:, base(L, 32), :], 1.0, spread(sc(C_N2, KD), 2, [P, KD]), ALU.add,
                    ALU.mult).then_inc(fact2, 1)
                for m in range(KD):
                    wout_residual(L, 1, m, m % 4)
                    if m == 3:
                        split_lo(L, N_WIN + 4, 0)
                rstd(L, L * RSTD + 6, ps[:, 7:8, 0:T], 1, 1.0 / D)
                normed(L, 1)

                def ffn_tile(i, j, width):
                    dve.wait_ge(silu_ready, L * N_F1 + i * 2 + (j + 1))
                    tt(nt[:, j, :], ny[:, j, :], ps[:, 2 * j + 1, 0:T], ALU.mult).then_inc(hid_ready, 1)
                    split_lo(L, (i, N_WIN + N_WOUT + j + 2), j, width)
                    dve.wait_ge(hid_hi_ready, L * N_F1 + i * 2 + (j + 1))
                    hk = bass.ds(i * 2 + j, 1)
                    tt(hid_lo[:, hk, :], nt[:, j:j + 1, :], hid_hi[:, hk, :].bitcast(F32), ALU.subtract)\
                        .then_inc(hid_lo_ready, 1)

                with dve.Fori(0, L * 2 + (N_F1 // 2 - 4)) as i:
                    for j in range(2):
                        ffn_tile(i, j, BLK)
                with dve.Fori(0, 3 - L * 2) as t:
                    i, p, turn = beside_ffn(L, t)
                    ffn_tile(i, 0, BLK)
                    ada_rows(p)
                    ffn_tile(i, 1, BLK)
                    ada_mod(turn, p, bank=5)
                dve.wait_ge(mod_ready, L * TURNS + 5)
                nc.vector.tensor_copy(modl[:, 40:48, :], mod[:, base(L, 40), :]).then_inc(gate2_ready, 1)
                dve.wait_ge(gate2_ready, L + 1)
                for j in range(2):
                    ffn_tile(N_F1 // 2 - 1, j, F2BLK)

                def ffn_out(i, m, more):
                    for j in range(2):
                        k = 2 * m + j + N_WIN + N_WOUT + N_F1
                        if m == 0 or more:
                            dve.wait_ge(w_hi, L * NB + i * 4 + (k + 3))
                            tt(wlo[:, j, 0:F2BLK], stage[:, j, 0:F2BLK], whi[:, j, 0:F2BLK].bitcast(F32),
                               ALU.subtract).then_inc(w_split, 1)
                    dve.wait_ge(w_used, L * NB + i * 4 + (2 * m + 1 + N_WIN + N_WOUT + N_F1 + 3))
                    residual(L, m, i * 2 + m, 40)

                with dve.Fori(0, KD // 2 - 1) as i:
                    for m in range(2):
                        ffn_out(i, m, True)
                for m in range(2):
                    ffn_out(KD // 2 - 1, m, False)
            assert steps[0] == DVE_STEPS, steps[0]
            steps[0] = DVE_STEPS * DEPTH
            rstd(None, RSTD * DEPTH + 1, ps[:, 7:8, 0:T], 1, 1.0 / D)
            for k in range(KD):
                stt(sq[:, k, :], x[:, k, :], cc(K_FN + k, 1), nv[:, 0, :], ALU.mult, ALU.mult).then_inc(y_ready, 1)

        @block.gpsimd
        def _(pool):
            g = nc.gpsimd
            dtv = dts[:, 0:48].rearrange("p (c d h) -> p c d h", c=NCH, d=2)
            def split_lo(L, n, j):
                pool.wait_ge(w_split, L * NB + n + 2)
                pool.wait_ge(w_hi, L * NB + n + 1)
                g.tensor_tensor(wlo[:, j, :], stage[:, j, :], whi[:, j, :].bitcast(F32), ALU.subtract)\
                    .then_inc(w_split, 1)

            with pool.Fori(0, DEPTH) as L:
                for n in (1, 2, 4, 5):
                    split_lo(L, n, n % 2)
                pool.wait_ge(tedt_ready, L * 2 + 2)
                pool.wait_ge(tr_ready, L * 4 + 4)
                h8 = "p (h n) -> p h n"
                for s, (c, d) in enumerate(STATE_JOBS):
                    g.tensor_tensor(vte[s].rearrange(h8, h=HS), xt[:, c, :].rearrange(h8, h=HS),
                                    spread(tedt[:, d, c, :], 64, [P, HS]), ALU.mult).then_inc(vte_ready, 1)
                for c in range(NCH):
                    if c == 0:
                        pool.wait_ge(st_ps, L * 4 + 4)
                    else:
                        pool.wait_ge(y_ps, L * 6 + 2 * c)
                    for d in range(2):
                        g.tensor_tensor(vd[:, d].rearrange(h8, h=HS), xt[:, c, :].rearrange(h8, h=HS),
                                        spread(dtv[:, c, d, :], 64, [P, HS]), ALU.mult).then_inc(vd_ready, 1)
                pool.wait_ge(rmat_ready, L * 2 + 2)
                pool.wait_ge(kv_ready, L * 3 + 3)
                pool.wait_ge(prob_ready, L * 12 + 12)
                for s, (c, d) in enumerate(STATE_JOBS):
                    if s >= 2:
                        pool.wait_ge(rst_ps, L * 4 + s - 1)
                    g.tensor_tensor(vtr[s % 2].rearrange(h8, h=HR), kvt[:, c, 256:512].rearrange(h8, h=HR),
                                    spread(ter[:, d, :], 64, [P, HR]), ALU.mult).then_inc(rvt_ready, 1)
                pool.wait_ge(y_ps, L * 6 + 6)
                for c in range(1, NCH):
                    if c > 1:
                        pool.wait_ge(ry_ps, L * 3 + c)
                    for d in range(2):
                        g.tensor_tensor(qr[:, d], u[:, U_RQ:U_RQ + 2, c * P:c * P + P], rq[d], ALU.mult)\
                            .then_inc(qr_ready, 1)
                split_lo(L, N_WIN + 5, 1)


def constants(b_ada, final_w, conds):
    a = np.zeros((P, CONSTW), np.float32)
    t = np.arange(P)
    a[:, K_ID:K_ID + P] = np.eye(P)
    a[:, K_U:K_U + P] = t[:, None] <= t
    a[:, K_L:K_L + P] = t[:, None] >= t
    a[:, K_SU:K_SU + P] = t[:, None] < t
    a[:, K_SL:K_SL + P] = t[:, None] > t
    a[:, K_BD:K_BD + P] = (t[:, None] // 64 == t // 64) / 64.0
    a[:, K_ONE:K_ONE + P] = 1.0
    a[:, K_PF:K_PF + P] = np.maximum(t - t[:, None], 0)
    a[:, K_PB:K_PB + P] = np.maximum(t[:, None] - t, 0)
    a[:, K_IP:K_IP + P] = t + 1
    a[:, K_IB:K_IB + P] = P - t
    a[:, K_PC], a[:, K_PC + 1] = P - 1 - t, t
    a[:, K_EPS] = EPS
    half = ROPE // 2
    inv = np.float32(10000.0) ** (-np.arange(0, half, 2, dtype=np.float32) / np.float32(half))
    pos = np.arange(LAT)
    ar = (pos // 64).astype(np.float32)[:, None] * inv
    ac = (pos % 64).astype(np.float32)[:, None] * inv
    ang = np.concatenate([ar, ar, ac, ac], 1).T
    a[KR0:KR0 + ROPE, K_COS:K_COS + LAT] = np.cos(ang)
    a[KR0:KR0 + ROPE, K_SIN:K_SIN + LAT] = np.sin(ang)
    for m in range(ROPE):
        if m % half < half // 2:
            a[KR0 + m + half // 2, K_PERM + KR0 + m] = -1.0
        else:
            a[KR0 + m - half // 2, K_PERM + KR0 + m] = 1.0
    a[:, K_BADA:K_BADA + DEPTH * 48] = b_ada
    a[:, K_FN:K_FN + KD] = final_w
    a[:, K_COND:K_COND + 2 * KD] = conds
    return a


OUTS = [(P, KD, T), (DEPTH, P, 512), (DEPTH, P, 256), (DEPTH, P, CTX), (DEPTH, ROPE, CTX)]


def kernel(x_prompt, x_sample, c, state_ssd, state_ret, cache_mla_ckv, cache_mla_krope, c_ctx, w_ada, b_ada, norm1_w,
           w_in, ssd_conv_w, ssd_conv_b, ssd_dt_bias, ssd_A_log, ssd_D, ssd_norm_w, ret_decay_logit, ret_gn_w,
           mla_q_norm_w, mla_w_uq, mla_kv_norm_w, mla_w_ukv, w_out, norm2_w, ffn_w1, ffn_w2, final_norm_w):
    import concourse.bacc as _bacc
    from concourse.bass_utils import run_bass_kernel_spmd as _run

    n = DEPTH
    cat = np.concatenate
    arr = np.asarray

    def tiles(a):
        a = arr(a)
        return np.moveaxis(a.reshape(*a.shape[:-1], -1, P), -1, -2)

    def blocks(a, width):
        a = arr(a)
        k, m = a.shape[1] // P, a.shape[2] // width
        return a.reshape(n, k, P, m, width).transpose(0, 3, 2, 1, 4).reshape(n, m, P, k * width)

    def everywhere(a):
        a = arr(a).reshape(n, 1, -1)
        return np.broadcast_to(a, (n, P, a.shape[2]))

    def by_rows(a):
        a = np.moveaxis(arr(a).reshape(n, -1, arr(a).shape[-1] // 2, 2), 1, 2)
        a = np.moveaxis(a, 3, 1).reshape(n, 2, -1)
        return np.repeat(a, 64, axis=1)

    xt = cat([arr(x_prompt)[0], arr(x_sample)[0]]).T.reshape(KD, P, T).transpose(1, 0, 2)
    w_in = arr(w_in)
    starts = (512, 768, 1024, 1296, 1552, 1808, 2320, None, 0, 256, 2064)
    cols = [w_in[:, :, s:s + 256] if s is not None else
            cat([w_in[:, :, 2576:2704], w_in[:, :, 2640:2736], np.zeros((n, D, 32), np.float32)], axis=2)
            for s in starts]
    win = blocks(cat(cols, axis=2), 256).reshape(n * (N_WIN - 1), P, BLK)
    wdt = blocks(w_in[:, :, 1280:1296], 16).reshape(n, P, P)
    wout = arr(w_out).reshape(n, 2, KW2, P, 2, 4, P).transpose(0, 1, 4, 3, 5, 2, 6).reshape(n * N_WOUT, P, BLK)
    f1 = arr(ffn_w1).reshape(n, D, 2, KF, P).transpose(0, 1, 3, 2, 4).reshape(n, D, 2 * DFF)
    wf1 = blocks(f1, 256).reshape(n * N_F1, P, BLK)
    wf2 = arr(ffn_w2).reshape(n, 2, KH2, P, KD, P).transpose(0, 4, 1, 3, 2, 5).reshape(n * N_F2, P, F2BLK)
    wada = arr(w_ada).reshape(n, KD, P, 6, D).transpose(0, 3, 1, 2, 4).reshape(n * 6 * KD, P, D)
    wada = wada[[p * KD + k for p, k in ada_order()]]

    kr = np.zeros((n, P, P), np.float32)
    kr[:, KR0:KR0 + ROPE] = arr(cache_mla_krope)[0].transpose(0, 2, 1)
    h0s = arr(state_ssd)[0].reshape(n, 2, 2, HSG, 64, 64).transpose(0, 2, 4, 1, 3, 5).reshape(n, P, 512)
    h0r = arr(state_ret)[0].reshape(n, 2, 2, 2, 64, 64).transpose(0, 3, 4, 1, 2, 5).reshape(n, P, 256)
    small = cat([
        tiles(norm1_w), tiles(norm2_w),
        tiles(ssd_conv_w).transpose(0, 2, 1, 3).reshape(n, P, -1), tiles(ssd_conv_b), tiles(ssd_norm_w),
        tiles(ret_gn_w), tiles(mla_q_norm_w), tiles(mla_kv_norm_w), by_rows(ssd_D),
        everywhere(ssd_dt_bias), everywhere(ssd_A_log), everywhere(ret_decay_logit), by_rows(ret_decay_logit),
        h0s, h0r, arr(cache_mla_ckv)[0].transpose(0, 2, 1), kr,
        arr(mla_w_uq).reshape(n, 2, P, 384).transpose(0, 2, 1, 3).reshape(n, P, 768), arr(mla_w_ukv)], axis=2)
    assert small.shape[2] == SMALLW
    conds = np.stack([tiles(arr(c_ctx)), tiles(arr(c)[0])], axis=-1).reshape(P, 2 * KD)
    const = constants(tiles(b_ada).transpose(1, 0, 2).reshape(P, n * 48), tiles(final_norm_w), conds)

    nc = _bacc.Bacc("TRN2", target_bir_lowering=False, num_devices=1)
    arrays, args = {}, []
    for name, a in dict(x=xt, const=const, small=small, win=win, wdt=wdt, wout=wout, wf1=wf1, wf2=wf2,
                        wada=wada).items():
        a = np.ascontiguousarray(a)
        arrays[f"{name}_dram"] = a
        args.append(nc.dram_tensor(f"{name}_dram", a.shape, mybir.dt.from_np(a.dtype), kind="ExternalInput").ap())
    for i, shape in enumerate(OUTS):
        args.append(nc.dram_tensor(f"out_{i}_dram", shape, F32, kind="ExternalOutput").ap())
    program(nc, *args)
    r = _run(nc, [arrays], core_ids=[0]).results[0]
    y, ss, sr, ckv, krope = (r[f"out_{i}_dram"] for i in range(len(OUTS)))
    y = y.transpose(2, 1, 0).reshape(T, D)
    ss = ss.reshape(n, 2, 64, 2, HSG, 64).transpose(0, 3, 1, 4, 2, 5).reshape(1, n, 2, HS, 64, 64)
    sr = sr.reshape(n, 2, 64, 2, 2, 64).transpose(0, 3, 4, 1, 2, 5).reshape(1, n, 2, HR, 64, 64)
    return (np.ascontiguousarray(y[:CTX])[None], np.ascontiguousarray(y[CTX:])[None], np.ascontiguousarray(ss),
            np.ascontiguousarray(sr), np.ascontiguousarray(ckv.transpose(0, 2, 1))[None],
            np.ascontiguousarray(krope.transpose(0, 2, 1))[None])
```
